# Optimizing a Trainium2 kernel written in Bass

```python
import numpy as np
import jax
import jax.numpy as jnp
from jax import lax

D_MODEL = 1024
BATCH = 1
SEQ = 512
DEPTH = 2

HEAD_DIM = 64
N_HEADS_A = D_MODEL // (2 * HEAD_DIM)
N_KV_GROUPS = 2
HEADS_PER_GROUP = N_HEADS_A // N_KV_GROUPS
A_WIDTH = N_HEADS_A * HEAD_DIM
KV_WIDTH = N_KV_GROUPS * HEAD_DIM
ROPE_DIM = HEAD_DIM // 4
ROPE_THETA = 500000.0
CMP_BLOCK = 32
CMP_STRIDE = 16
CMP_HIDDEN = 2 * HEAD_DIM
SEL_BLOCK = 64
SEL_TOPK = 16
WINDOW = 512
Q_CHUNK = 128
N_BRANCH = 3
CONV_WIDTH = 3
B_WIDTH = D_MODEL - A_WIDTH
P_IN = A_WIDTH + 6 * KV_WIDTH + N_BRANCH * N_HEADS_A + 3 * B_WIDTH
POOL_WINDOWS = (2, 4, 8, 16)
POOL_GROUP = D_MODEL // len(POOL_WINDOWS)
D_FF = 2816
N_EVEN = (DEPTH + 1) // 2
N_ODD = DEPTH // 2
EPS = 1e-6
NEG = -1e30

kernel_name = 'hybrid_nsa_shortconv_pool_macaron'

def rms_norm(x, g):
    xf = x.astype(jnp.float32)
    y = xf * lax.rsqrt(jnp.mean(xf * xf, axis=-1, keepdims=True) + EPS)
    return (y * g.astype(jnp.float32)).astype(x.dtype)

def swiglu(h, wg, wu, wd):
    return (jax.nn.silu(h @ wg) * (h @ wu)) @ wd

def rope_tables(pos):
    freqs = ROPE_THETA ** (-jnp.arange(0, ROPE_DIM, 2, dtype=jnp.float32) / ROPE_DIM)
    ang = pos.astype(jnp.float32)[..., None] * freqs
    return jnp.cos(ang), jnp.sin(ang)

def apply_partial_rope(x, cos, sin):
    half = ROPE_DIM // 2
    shp = cos.shape[:2] + (1,) * (x.ndim - 3) + (half,)
    c = cos.reshape(shp)
    s = sin.reshape(shp)
    xf = x.astype(jnp.float32)
    x1, x2, rest = xf[..., :half], xf[..., half:ROPE_DIM], xf[..., ROPE_DIM:]
    out = jnp.concatenate([x1 * c - x2 * s, x2 * c + x1 * s, rest], axis=-1)
    return out.astype(x.dtype)

def cmp_block_index(seq):
    n_cmp = (seq - CMP_BLOCK) // CMP_STRIDE + 1
    return np.arange(n_cmp)[:, None] * CMP_STRIDE + np.arange(CMP_BLOCK)[None, :]

def compress(kv, pos_emb, w1, w2, idx):
    bsz = kv.shape[0]
    blocks = kv[:, idx] + pos_emb[None, None, :, None, :]
    blocks = blocks.transpose(0, 1, 3, 2, 4).reshape(bsz, idx.shape[0], N_KV_GROUPS, CMP_BLOCK * HEAD_DIM)
    return jax.nn.gelu(blocks @ w1) @ w2

def masked_softmax(s, mask):
    return jax.nn.softmax(jnp.where(mask, s.astype(jnp.float32), NEG), axis=-1)

def nsa_core(q, kc, vc, ks, vs, kw, vw, gates, blk_end):
    bsz, seq = q.shape[0], q.shape[1]
    n_chunks = seq // Q_CHUNK
    n_sel = seq // SEL_BLOCK
    k_eff = min(SEL_TOPK, n_sel)
    scale = HEAD_DIM ** -0.5
    G, Hg, d = N_KV_GROUPS, HEADS_PER_GROUP, HEAD_DIM

    cmp_start = np.arange(blk_end.shape[0]) * CMP_STRIDE
    sel_start_np = np.arange(n_sel) * SEL_BLOCK
    overlap = jnp.asarray(((cmp_start[:, None] < sel_start_np[None, :] + SEL_BLOCK)
                           & (cmp_start[:, None] + CMP_BLOCK > sel_start_np[None, :])).astype(np.float32))
    sel_start = jnp.asarray(sel_start_np)
    blk_end_j = jnp.asarray(blk_end)

    ks_blocks = ks.reshape(bsz, n_sel, SEL_BLOCK, G, d).transpose(0, 3, 1, 2, 4)
    vs_blocks = vs.reshape(bsz, n_sel, SEL_BLOCK, G, d).transpose(0, 3, 1, 2, 4)
    kw_pad = jnp.pad(kw, ((0, 0), (WINDOW, 0), (0, 0), (0, 0)))
    vw_pad = jnp.pad(vw, ((0, 0), (WINDOW, 0), (0, 0), (0, 0)))
    gather_blocks = jax.vmap(jax.vmap(lambda blocks, ix: blocks[ix]))

    def chunk(args):
        c, q_c, g_c = args
        t = c * Q_CHUNK + jnp.arange(Q_CHUNK)

        s = jnp.einsum('bqghd,bngd->bghqn', q_c, kc) * scale
        valid = blk_end_j[None, :] <= t[:, None]
        p_cmp = masked_softmax(s, valid) * jnp.any(valid, axis=-1)[:, None].astype(jnp.float32)
        o_cmp = jnp.einsum('bghqn,bngd->bqghd', p_cmp.astype(vc.dtype), vc)

        imp = jnp.einsum('bghqn,nm->bgqm', p_cmp, overlap)
        cur = (t // SEL_BLOCK) * SEL_BLOCK
        forced = (sel_start[None, :] == cur[:, None]) | (sel_start[None, :] == 0)
        imp = jnp.where(sel_start[None, :] <= t[:, None], imp, -1.0)
        imp = jnp.where(forced, 1e4, imp)
        _, sel = lax.top_k(imp, k_eff)
        kg = gather_blocks(ks_blocks, sel)
        vg = gather_blocks(vs_blocks, sel).reshape(bsz, G, Q_CHUNK, k_eff * SEL_BLOCK, d)
        kpos = sel[..., None] * SEL_BLOCK + jnp.arange(SEL_BLOCK)
        mask_s = (kpos <= t[:, None, None]).reshape(bsz, G, 1, Q_CHUNK, k_eff * SEL_BLOCK)
        s = jnp.einsum('bqghd,bgqksd->bghqks', q_c, kg) * scale
        s = s.reshape(bsz, G, Hg, Q_CHUNK, k_eff * SEL_BLOCK)
        p = masked_softmax(s, mask_s)
        o_slc = jnp.einsum('bghqj,bgqjd->bqghd', p.astype(vg.dtype), vg)

        kwc = lax.dynamic_slice_in_dim(kw_pad, c * Q_CHUNK, WINDOW + Q_CHUNK, axis=1)
        vwc = lax.dynamic_slice_in_dim(vw_pad, c * Q_CHUNK, WINDOW + Q_CHUNK, axis=1)
        kpos_w = c * Q_CHUNK - WINDOW + jnp.arange(WINDOW + Q_CHUNK)
        diff = t[:, None] - kpos_w[None, :]
        mask_w = (diff >= 0) & (diff < WINDOW) & (kpos_w[None, :] >= 0)
        s = jnp.einsum('bqghd,bkgd->bghqk', q_c, kwc) * scale
        p = masked_softmax(s, mask_w)
        o_win = jnp.einsum('bghqk,bkgd->bqghd', p.astype(vwc.dtype), vwc)

        return g_c[..., 0:1] * o_cmp + g_c[..., 1:2] * o_slc + g_c[..., 2:3] * o_win

    q_chunks = q.reshape(bsz, n_chunks, Q_CHUNK, G, Hg, d).swapaxes(0, 1)
    g_chunks = gates.reshape(bsz, n_chunks, Q_CHUNK, G, Hg, N_BRANCH).swapaxes(0, 1)
    out = lax.map(chunk, (jnp.arange(n_chunks), q_chunks, g_chunks))
    return out.swapaxes(0, 1).reshape(bsz, seq, A_WIDTH)

def causal_shift(v, n):
    return jnp.pad(v, ((0, 0), (n, 0), (0, 0)))[:, :v.shape[1]]

def hybrid_mixer(h, positions, w_in, q_norm, k_norm, cmp_pos, cmp_w1, cmp_w2, conv_w, w_out):
    bsz, seq, _ = h.shape
    G, Hg, d = N_KV_GROUPS, HEADS_PER_GROUP, HEAD_DIM
    proj = h @ w_in
    sizes = [A_WIDTH] + [KV_WIDTH] * 6 + [N_BRANCH * N_HEADS_A] + [B_WIDTH] * 3
    q, kc, vc, ks, vs, kw, vw, gates, u, gate_b, gate_c = jnp.split(
        proj, np.cumsum(sizes)[:-1].tolist(), axis=-1)

    cos, sin = rope_tables(positions)
    q = apply_partial_rope(rms_norm(q.reshape(bsz, seq, G, Hg, d), q_norm), cos, sin)
    ks = apply_partial_rope(rms_norm(ks.reshape(bsz, seq, G, d), k_norm[1]), cos, sin)
    kw = apply_partial_rope(rms_norm(kw.reshape(bsz, seq, G, d), k_norm[2]), cos, sin)
    vs = vs.reshape(bsz, seq, G, d)
    vw = vw.reshape(bsz, seq, G, d)
    idx = cmp_block_index(seq)
    blk_end = idx[:, -1]
    kc = compress(kc.reshape(bsz, seq, G, d), cmp_pos[0], cmp_w1[0], cmp_w2[0], idx)
    vc = compress(vc.reshape(bsz, seq, G, d), cmp_pos[1], cmp_w1[1], cmp_w2[1], idx)
    cos_c, sin_c = rope_tables(positions[:, blk_end])
    kc = apply_partial_rope(rms_norm(kc, k_norm[0]), cos_c, sin_c)
    gates = jax.nn.sigmoid(gates.astype(jnp.float32)).reshape(bsz, seq, G, Hg, N_BRANCH).astype(h.dtype)
    o_a = nsa_core(q, kc, vc, ks, vs, kw, vw, gates, blk_end)

    v = gate_c * u
    y = conv_w[2] * v + conv_w[1] * causal_shift(v, 1) + conv_w[0] * causal_shift(v, 2)
    o_b = gate_b * y

    return jnp.concatenate([o_a, o_b], axis=-1) @ w_out

def pool_mixer(h, w, scale):
    seq = h.shape[1]
    hf = h.astype(jnp.float32)
    cs = jnp.concatenate([jnp.zeros_like(hf[:, :1]), jnp.cumsum(hf, axis=1)], axis=1)
    t = np.arange(seq)
    outs = []
    for gi, win in enumerate(POOL_WINDOWS):
        sl = slice(gi * POOL_GROUP, (gi + 1) * POOL_GROUP)
        lo = np.maximum(t + 1 - win, 0)
        cnt = jnp.asarray(np.minimum(t + 1, win).astype(np.float32))
        mean = (cs[:, 1:, sl] - cs[:, lo, sl]) / cnt[None, :, None]
        outs.append((mean - hf[..., sl]).astype(h.dtype) @ w[gi])
    return jnp.concatenate(outs, axis=-1) * scale

def setup_inputs(seed: int = 0) -> dict:
    key = jax.random.key(seed)
    ks = jax.random.split(key, 20)
    f32 = jnp.float32

    def nrm(k, shape, fan_in):
        return jax.random.normal(k, shape, f32) * (fan_in ** -0.5)

    def gain(k, shape):
        return 1.0 + 0.02 * jax.random.normal(k, shape, f32)

    x = jax.random.normal(ks[0], (BATCH, SEQ, D_MODEL), f32)
    positions = jnp.broadcast_to(jnp.arange(SEQ, dtype=jnp.int32), (BATCH, SEQ))
    return {
        'x': x,
        'positions': positions,
        'ffn_norm': gain(ks[1], (DEPTH, 2, D_MODEL)),
        'ffn_w_gate': nrm(ks[2], (DEPTH, 2, D_MODEL, D_FF), D_MODEL),
        'ffn_w_up': nrm(ks[3], (DEPTH, 2, D_MODEL, D_FF), D_MODEL),
        'ffn_w_down': nrm(ks[4], (DEPTH, 2, D_FF, D_MODEL), D_FF),
        'mix_norm': gain(ks[5], (DEPTH, D_MODEL)),
        'hyb_w_in': nrm(ks[6], (N_EVEN, D_MODEL, P_IN), D_MODEL),
        'hyb_q_norm': gain(ks[7], (N_EVEN, HEAD_DIM)),
        'hyb_k_norm': gain(ks[8], (N_EVEN, N_BRANCH, HEAD_DIM)),
        'hyb_cmp_pos': 0.02 * jax.random.normal(ks[9], (N_EVEN, 2, CMP_BLOCK, HEAD_DIM), f32),
        'hyb_cmp_w1': nrm(ks[10], (N_EVEN, 2, CMP_BLOCK * HEAD_DIM, CMP_HIDDEN), CMP_BLOCK * HEAD_DIM),
        'hyb_cmp_w2': nrm(ks[11], (N_EVEN, 2, CMP_HIDDEN, HEAD_DIM), CMP_HIDDEN),
        'hyb_conv_w': nrm(ks[12], (N_EVEN, CONV_WIDTH, B_WIDTH), CONV_WIDTH),
        'hyb_w_out': nrm(ks[13], (N_EVEN, A_WIDTH + B_WIDTH, D_MODEL), A_WIDTH + B_WIDTH),
        'pool_w': nrm(ks[14], (N_ODD, len(POOL_WINDOWS), POOL_GROUP, POOL_GROUP), POOL_GROUP),
        'pool_scale': 0.5 + 0.05 * jax.random.normal(ks[15], (N_ODD, D_MODEL), f32),
    }

def reference(x, positions, ffn_norm, ffn_w_gate, ffn_w_up, ffn_w_down, mix_norm,
              hyb_w_in, hyb_q_norm, hyb_k_norm, hyb_cmp_pos, hyb_cmp_w1, hyb_cmp_w2,
              hyb_conv_w, hyb_w_out, pool_w, pool_scale):
    for layer in range(DEPTH):
        h = rms_norm(x, ffn_norm[layer, 0])
        x = x + 0.5 * swiglu(h, ffn_w_gate[layer, 0], ffn_w_up[layer, 0], ffn_w_down[layer, 0])
        h = rms_norm(x, mix_norm[layer])
        i = layer // 2
        if layer % 2 == 0:
            x = x + hybrid_mixer(h, positions, hyb_w_in[i], hyb_q_norm[i], hyb_k_norm[i],
                                 hyb_cmp_pos[i], hyb_cmp_w1[i], hyb_cmp_w2[i],
                                 hyb_conv_w[i], hyb_w_out[i])
        else:
            x = x + pool_mixer(h, pool_w[i], pool_scale[i])
        h = rms_norm(x, ffn_norm[layer, 1])
        x = x + 0.5 * swiglu(h, ffn_w_gate[layer, 1], ffn_w_up[layer, 1], ffn_w_down[layer, 1])
    return x


_drawn_inputs = setup_inputs


def setup_inputs(seed=0):
    import zlib

    import numpy as np

    out = dict(_drawn_inputs(seed))
    spreads = {}
    factors = {'ffn_norm': 3.444,
     'hyb_q_norm': 8.0,
     'hyb_k_norm': 8.0,
     'hyb_cmp_pos': 8.0,
     'pool_scale': 8.0}
    for name, (base, spread) in spreads.items():
        noise = np.random.default_rng([zlib.crc32(name.encode()), seed]).standard_normal(out[name].shape)
        drawn = base * np.exp(spread * noise) if base else spread * noise
        out[name] = jnp.asarray(drawn.astype(out[name].dtype))
    for name, factor in factors.items():
        out[name] = (out[name] * factor).astype(out[name].dtype)
    return out
```

```python
from contextlib import ExitStack

import numpy as np

import concourse.bass as bass
from concourse import mybir

F32 = mybir.dt.float32
F32R = mybir.dt.float32r
BF16 = mybir.dt.bfloat16
I32 = mybir.dt.int32
ALU = mybir.AluOpType
ACT = mybir.ActivationFunctionType
AX_X = mybir.AxisListType.X

P = 128
T = 512
D = 1024
KD = D // P
F = 2816
KF = F // P
KH2 = KF // 2
DH = 64
HEADS = 8
NQ = 4
NC = 31
NCP = 32
EPS = 1e-6
NEG = -1e30
TE = T + 16
PW = 2 * TE

COL_Q, COL_KC, COL_VC, COL_KS, COL_VS, COL_KW, COL_VW, COL_G = 0, 512, 640, 768, 896, 1024, 1152, 1280
COL_U = COL_G + 24
COL_GB = COL_U + 512
COL_GC = COL_GB + 512

U_FFN = {0: 0}
U_MIX = U_FFN[0] + 2 * KF + 2 * KD
U_W1 = U_MIX + 7
U_LOOP = U_W1 + 4
U_OUT = U_LOOP + 16
U_FFN[1] = U_OUT + KD
U_FFN[2] = U_FFN[1] + 2 * KF + 2 * KD
U_POOL = U_FFN[2] + 2 * KF + 2 * KD
U_FFN[3] = U_POOL + 4
U_END = U_FFN[3] + 2 * KF + 2 * KD

BLOCKS = [KD] * U_END
DMAS = [1] * U_END
for ffn in range(4):
    for u in range(2 * KD):
        BLOCKS[U_FFN[ffn] + 2 * KF + u] = KH2
for u in range(4):
    BLOCKS[U_POOL + u] = 4
    DMAS[U_LOOP + 4 * u] = 2
for u in range(KD):
    DMAS[U_OUT + u] = 3


def landed_by(n):
    return 16 * sum(DMAS[m] for m in range(n % 4, n + 1, 4))


XG_OF = {0: 0, 1: 1, 2: 2, 3: 3, 5: 4}
LATE = NQ


def tile_order(version):
    return [*range(LATE, KD), *range(LATE)] if version == 2 else [*range(KD)]


STATS = ["x0", "x1", "ks", "kw", "q0", "q1", "q2", "kc", "q3", "x2", "x3", "x4", "x5"]
AUX = ["rows", "pos", "rot_ks", "rot_kw", "t_vs", "t_vw", "t_gates", "rot_q0", "rot_q1", "rot_q2", "w2", "rot_kc",
       "t_vc", "rot_q3"]

R_FFN, R_MIX, R_PSC, R_CONV, R_QN, R_KN, R_POS, N_ROWS = 0, 32, 48, 56, 68, 69, 72, 104

C_ID, C_ONE, C_BLK, C_ROT, C_MASK = 0, 128, 256, 384, 512
C_CMASK = 640
C_FREQ = 768
C_VALID = 769
C_POOL = 770
N_CONST = C_POOL + 64


def shape_constants():
    c = np.zeros((P, N_CONST), np.float32)
    r = np.arange(P)
    c[:, C_ID:C_ID + P] = np.eye(P)
    c[:, C_ONE:C_ONE + P] = 1.0
    c[:, C_BLK:C_BLK + P] = (r[:, None] // DH == r[None, :] // DH)
    for d in range(P):
        if d % DH < 8:
            c[d + 8, C_ROT + d] = -1.0
        elif d % DH < 16:
            c[d - 8, C_ROT + d] = 1.0
        if d % DH < 16:
            c[d, C_FREQ] = 500000.0 ** (-(d % 8) * 2 / 16)
    c[:, C_MASK:C_MASK + P] = np.where(r[None, :] > r[:, None], NEG, 0.0)
    n = np.arange(NCP)
    for q in range(NQ):
        bad = (16 * n[None, :] + 31 > q * P + r[:, None]) | (n[None, :] >= NC)
        c[:, C_CMASK + q * NCP:C_CMASK + (q + 1) * NCP] = np.where(bad, NEG, 0.0)
    c[:, C_VALID] = r >= 31
    for g, w in enumerate((2, 4, 8, 16)):
        c[:, C_POOL + 16 * g:C_POOL + 16 * g + 16] = w / np.minimum(np.arange(16) + 1, w)
    return c


def circle_parts():
    out, rest = [], 2 * np.pi
    for bits in (9, 20):
        part = np.floor(rest * 2.0 ** bits) / 2.0 ** bits
        out.append(float(part))
        rest -= part
    return out + [float(np.float32(rest))]


PI_PARTS = circle_parts()
ROUND = 1.5 * 2.0 ** 23


def at_least(eng, sem, value):
    if isinstance(value, int) and value <= 0:
        return
    eng.wait_ge(sem, value)


def build(nc, A, out):
    with ExitStack() as ctx:
        def sb(name, shape, dt=F32, where=ctx):
            return where.enter_context(nc.sbuf_tensor(name, shape, dt))

        def sem(name):
            return ctx.enter_context(nc.semaphore(name))

        consts = sb("consts", [P, N_CONST])
        ident_b = sb("ident_b", [P, P], BF16)
        mask_b = sb("mask_b", [P, P + NQ * NCP], BF16)
        cols = sb("cols", [P, N_ROWS])
        x_t = sb("x_t", [P, KD * T])
        xg_hi = sb("xg_hi", [P, KD * T], F32R)
        xg_lo = sb("xg_lo", [P, KD * T], F32R)
        raw = sb("raw", [P, 4, KH2 * P])
        w_hi = sb("w_hi", [P, 2, KH2 * P], F32R)
        w_lo = sb("w_lo", [P, 2, KH2 * P], F32R)
        work = sb("work", [P, 2, T])
        scratch = sb("scratch", [P, 4, T])
        work2, sq, ss, ms = (scratch[:, i, :] for i in range(4))
        rstd = sb("rstd", [P, T])
        cos_t = sb("cos_t", [P, TE])
        sin_t = sb("sin_t", [P, TE])
        w2_raw = sb("w2_raw", [P, 2, 2, DH])
        half = sb("half", [P, 1])
        ang, turns, step_ = sin_t[:, 0:T], cos_t[:, 0:T], ss[:, :]
        eps_col = sb("eps_col", [P, 1])

        with ExitStack() as once:
            rows = sb("rows", [N_ROWS, P], F32, once)
            x_in = sb("x_in", [P, NQ, D], F32, once)
            pos_i = sb("pos_i", [1, T], I32, once)
            pos_f = sb("pos_f", [1, T], F32, once)
        with ExitStack() as ffn_ctx:
            act_hi = sb("act_hi", [P, KF * T], F32R, ffn_ctx)
            act_lo = sb("act_lo", [P, KF * T], F32R, ffn_ctx)
        with ExitStack() as mix_ctx:
            def mb(name, shape, dt=F32):
                return sb(name, shape, dt, mix_ctx)
            qf = mb("qf", [P, NQ * T])
            q_parts = mb("q_parts", [P, 2, T], F32R)
            k_hi = mb("k_hi", [P, 2, 2, T], F32R)
            k_lo = mb("k_lo", [P, 2, 2, T], F32R)
            kc_hi = mb("kc_hi", [P, 2, NCP], F32R)
            kc_lo = mb("kc_lo", [P, 2, NCP], F32R)
            v_hi = mb("v_hi", [P, 2, NQ * P], F32R)
            v_lo = mb("v_lo", [P, 2, NQ * P], F32R)
            vc_hi = mb("vc_hi", [NCP, P], F32R)
            vc_lo = mb("vc_lo", [NCP, P], F32R)
            ob_hi = mb("ob_hi", [P, 4 * T], F32R)
            ob_lo = mb("ob_lo", [P, 4 * T], F32R)
            prob = mb("prob", [P, 2, PW])
            pt_b = mb("pt_b", [P, 2, 4 * T], F32R)
            prob_c = mb("prob_c", [P, NQ, NCP])
            ptc = mb("ptc", [NCP, 2, T], F32R)
            m1 = mb("m1", [P, T])
            vt = mb("vt", [P, T])
            hid = mb("hid", [P, 2, 2, DH])
            hid_hi = mb("hid_hi", [P, 2, DH], F32R)
            hid_lo = mb("hid_lo", [P, 2, DH], F32R)
            kcv = mb("kcv", [P, 2, DH])
            kcm = mb("kcm", [P, 2, DH])
            gate = mb("gate", [P, 2, NQ * 24])
            small = mb("small", [P, 2, 10])
            small_c = mb("small_c", [P, 5, NQ])
            w2_hi, w2_lo = (q_parts[:, i, 0:2 * P].rearrange("p (c d) -> p c d", c=2) for i in range(2))
        with ExitStack() as pool_ctx:
            h_pad = sb("h_pad", [P, KD, TE], F32, pool_ctx)
            sum_a = sb("sum_a", [P, 2, TE], F32, pool_ctx)
            sum_b = sb("sum_b", [P, 2, TE], F32, pool_ctx)
            diff = sb("diff", [P, 2, 2 * T], F32, pool_ctx)

        ps_s = ctx.enter_context(nc.psum_tensor("ps_s", [P, 4, T], F32))
        ps_y = ctx.enter_context(nc.psum_tensor("ps_y", [P, 2, T], F32))
        ps_stat = ctx.enter_context(nc.psum_tensor("ps_stat", [P, T], F32))
        ps_aux = ctx.enter_context(nc.psum_tensor("ps_aux", [P, T], F32))

        raw_landed = [sem(f"raw_landed{i}") for i in range(4)]
        const_landed = sem("const_landed")
        rows_landed = sem("rows_landed")
        w2_landed = sem("w2_landed")
        x_landed = [sem(f"x_landed{i}") for i in range(NQ)]
        hi_ready = sem("hi_ready")
        lo_ready = sem("lo_ready")
        unit_done = sem("unit_done")
        rows_turned = sem("rows_turned")
        x_turned = sem("x_turned")
        consts_cast = sem("consts_cast")
        x_ready = sem("x_ready")
        xg_hi_ready = sem("xg_hi_ready")
        xg_lo_ready = sem("xg_lo_ready")
        sq_ready = sem("sq_ready")
        ss_step = sem("ss_step")
        stat_done = sem("stat_done")
        ms_ready = sem("ms_ready")
        root_ready = sem("root_ready")
        gate_scaled = sem("gate_scaled")
        up_scaled = sem("up_scaled")
        silu_ready = sem("silu_ready")
        a_ready = sem("a_ready")
        act_hi_ready = sem("act_hi_ready")
        act_lo_ready = sem("act_lo_ready")
        aux_done = sem("aux_done")
        aux_free = sem("aux_free")
        pos_ready = sem("pos_ready")
        pool_step = sem("pool_step")
        pos_landed = sem("pos_landed")
        pair_step = sem("pair_step")
        max_step = sem("max_step")
        sum_step = sem("sum_step")
        pool_zeroed = sem("pool_zeroed")
        kc_hi_ready = sem("kc_hi_ready")
        conv_step = sem("conv_step")
        kc_ready = sem("kc_ready")
        turn_ready = sem("turn_ready")
        trig_ready = sem("trig_ready")
        mix_zeroed = sem("mix_zeroed")
        proj_scaled = sem("proj_scaled")
        head_sq = sem("head_sq")
        gained = sem("gained")
        m1_ready = sem("m1_ready")
        rope_ready = sem("rope_ready")
        dve_step = sem("dve_step")
        k_hi_ready = sem("k_hi_ready")
        k_lo_ready = sem("k_lo_ready")
        v_hi_ready = sem("v_hi_ready")
        blk_step = sem("blk_step")
        blk_hi_ready = sem("blk_hi_ready")
        blk_lo_ready = sem("blk_lo_ready")
        w2_hi_ready = sem("w2_hi_ready")
        w2_lo_ready = sem("w2_lo_ready")
        gelu_in = sem("gelu_in")
        gelu_tanh = sem("gelu_tanh")
        hid_ready = sem("hid_ready")
        hid_hi_ready = sem("hid_hi_ready")
        hid_lo_ready = sem("hid_lo_ready")
        gate_exp = sem("gate_exp")
        ob_ready = sem("ob_ready")
        ob_hi_ready = sem("ob_hi_ready")
        ob_lo_ready = sem("ob_lo_ready")
        qp_hi_ready = sem("qp_hi_ready")
        qp_lo_ready = sem("qp_lo_ready")
        qk_done = sem("qk_done")
        negmax_ready = sem("negmax_ready")
        exp_done = sem("exp_done")
        scale_ready = sem("scale_ready")
        pt_done = sem("pt_done")
        c_qk_done = sem("c_qk_done")
        c_max_step = sem("c_max_step")
        c_negmax_ready = sem("c_negmax_ready")
        c_exp_done = sem("c_exp_done")
        c_sum_step = sem("c_sum_step")
        c_scale_ready = sem("c_scale_ready")
        c_p_scaled = sem("c_p_scaled")
        c_pt_done = sem("c_pt_done")
        c_pt_hi_ready = sem("c_pt_hi_ready")
        c_pt_lo_ready = sem("c_pt_lo_ready")
        pt_hi_ready = sem("pt_hi_ready")
        pt_lo_ready = sem("pt_lo_ready")
        pv_done = sem("pv_done")
        o_hi_ready = sem("o_hi_ready")
        o_lo_ready = sem("o_lo_ready")
        h_ready = sem("h_ready")
        diff_ready = sem("diff_ready")
        diff_hi_ready = sem("diff_hi_ready")
        diff_lo_ready = sem("diff_lo_ready")
        out_turned = sem("out_turned")
        out_copied = sem("out_copied")
        out_stored = [sem(f"out_stored{i}") for i in range(2)]

        ident = consts[:, C_ID:C_ID + P]
        ones = consts[:, C_ONE:C_ONE + P]
        block_ones = consts[:, C_BLK:C_BLK + P]
        rot = consts[:, C_ROT:C_ROT + P]
        freq = consts[:, C_FREQ:C_FREQ + 1]

        def tile_of(tensor, d):
            return tensor[:, bass.ds(d * T, T)]

        def head_tiles(name):
            return STATS.index(name) - STATS.index("ks") + 1

        def turned_parts(slot_):
            if slot_:
                return pt_b[:, 0, :], pt_b[:, 1, :]
            return xg_hi[:, 4 * T:8 * T], xg_lo[:, 4 * T:8 * T]

        def prob_of(s):
            if s % 4 < 2:
                return prob[:, s % 4, :]
            return scratch[:, 2 * (s % 4) - 4:2 * (s % 4) - 2, :].rearrange("p b k -> p (b k)")

        def diagonal(s, br):
            return work[:, s % 2, br * P:(br + 1) * P]

        def f32(ap):
            return ap.bitcast(F32)

        block = ctx.enter_context(nc.Block())

        @block.sync
        def _(sp):
            for q in range(NQ):
                sp.dma_start(x_in[:, q, :], A["x"][0, q * P:(q + 1) * P, :]).then_inc(x_landed[q], 16)

            def load(n, i, *parts):
                at_least(sp, lo_ready, n - 3 + 4 * i)
                for dst, src in parts:
                    sp.dma_start(dst, src).then_inc(raw_landed[n % 4], 16)

            def slot(n, blocks=KD):
                return raw[:, n % 4, 0:blocks * P].rearrange("p (k f) -> p k f", f=P)

            def blocks_of(w):
                return w.rearrange("(k p) f -> p k f", p=P)

            def load_up(ffn, i):
                for u in range(4):
                    n, f = U_FFN[ffn] + u, 2 * i + u // 2
                    w = A["ffn_w_up" if u % 2 else "ffn_w_gate"][ffn // 2, ffn % 2]
                    load(n, i, (slot(n), blocks_of(w[:, bass.ds(f * P, P)])))

            def load_down(ffn, i):
                for u in range(4):
                    n, d, h = U_FFN[ffn] + 2 * KF + u, 2 * i + u // 2, u % 2
                    w = A["ffn_w_down"][ffn // 2, ffn % 2]
                    load(n, i, (slot(n, KH2), blocks_of(w[h * KH2 * P:(h + 1) * KH2 * P, bass.ds(d * P, P)])))

            def load_ffn(ffn):
                load_up(ffn, 0)
                with sp.Fori(1, KF // 2) as i:
                    load_up(ffn, i)
                with sp.Fori(0, KD // 2) as i:
                    load_down(ffn, i)

            load_ffn(0)
            w_in = A["hyb_w_in"][0]
            for u, col in enumerate((COL_KS, COL_KW, COL_KC, COL_VC, COL_VS, COL_VW, COL_G)):
                load(U_MIX + u, 0, (slot(U_MIX + u), blocks_of(w_in[:, col:col + P])))
            for u in range(4):
                w1 = A["hyb_cmp_w1"][0, u // 2][(u % 2) * KD * P:(u % 2 + 1) * KD * P, :]
                load(U_W1 + u, 0, (slot(U_W1 + u), blocks_of(w1)))
            with sp.Fori(0, 4) as i:
                for u, col in enumerate((COL_Q, COL_U, COL_GC, COL_GB)):
                    n = U_LOOP + u
                    if u == 0:
                        load(n, i, *((slot(n)[:, :, g * DH:(g + 1) * DH],
                                      blocks_of(w_in[:, bass.ds(i * DH + g * 4 * DH, DH)])) for g in range(2)))
                    else:
                        load(n, i, (slot(n), blocks_of(w_in[:, bass.ds(i * P + col, P)])))
            w_out = A["hyb_w_out"][0]
            for d in range(KD):
                n = U_OUT + d
                w = w_out[:, d * P:(d + 1) * P]
                load(n, 0, *((slot(n)[g * DH:(g + 1) * DH, 0:4, :],
                              w[g * 4 * DH:(g + 1) * 4 * DH, :].rearrange("(j p) f -> p j f", p=DH)) for g in range(2)),
                     (slot(n)[:, 4:8, :], blocks_of(w[T:2 * T, :])))
            load_ffn(1)
            load_ffn(2)
            for g in range(4):
                n = U_POOL + g
                load(n, 0, (raw[:, n % 4, 0:4 * P].rearrange("p (k f) -> p k f", k=2), blocks_of(A["pool_w"][0, g])))
            load_ffn(3)
            for d in range(KD):
                sp.wait_ge(out_copied, d + 1)
                sp.dma_start(out[0, :, d * P:(d + 1) * P].rearrange("(q p) f -> p q f", p=P),
                             work[:, d % 2, :].rearrange("p (q f) -> p q f", q=NQ)).then_inc(out_stored[d % 2], 16)
            for s in range(2):
                sp.wait_ge(out_stored[s], 16 * KD // 2)

        @block.tensor
        def _(pe):
            mm = nc.tensor.matmul

            def three(bank, hi, lo, x_hi, x_lo, first, last, **kw):
                mm(bank, hi, x_hi, start=first, stop=False, **kw)
                mm(bank, hi, x_lo, start=False, stop=False, **kw)
                return mm(bank, lo, x_hi, start=False, stop=last, **kw)

            def stat(index, weights, source, cols_=T):
                at_least(pe, ms_ready, index)
                mm(ps_stat[:, 0:cols_], weights, source, start=True, stop=True).then_inc(stat_done, 1)

            def unit(n, i, bank, x_hi, x_lo, k0=0, first=True, last=True, version=None):
                pe.wait_ge(lo_ready, n + 1 + 4 * i)
                order = range(BLOCKS[n]) if version is None else tile_order(version)
                for place, k in enumerate(order):
                    if version is not None:
                        pe.wait_ge(xg_lo_ready, KD * XG_OF[version] + place + 1)
                    last_mm = three(bank, w_hi[:, n % 2, k * P:(k + 1) * P], w_lo[:, n % 2, k * P:(k + 1) * P],
                                    tile_of(x_hi, k0 + k), tile_of(x_lo, k0 + k),
                                    first and place == 0, last and place == BLOCKS[n] - 1)
                last_mm.then_inc(unit_done, 1)

            def up(ffn, version, i, peeled):
                for u in range(4):
                    n, f = U_FFN[ffn] + u, 2 * i + u // 2
                    at_least(pe, up_scaled if u % 2 else gate_scaled, KF * ffn + f - 1)
                    fresh = peeled and u == 0
                    unit(n, i, ps_s[:, (u % 2) * 2 + u // 2, :], xg_hi, xg_lo,
                         version=version if fresh else None)
                    if fresh:
                        pe.wait_ge(ss_step, KD * (version + 1))
                        stat(STATS.index(f"x{version}"), ones, ss[:, :])

            def down(ffn, version_out, i):
                for u in range(4):
                    n, d, h = U_FFN[ffn] + 2 * KF + u, 2 * i + u // 2, u % 2
                    if h == 0:
                        pe.wait_ge(x_ready, KD * version_out + d - 1)
                    pe.wait_ge(act_lo_ready, KF * ffn + (h + 1) * KH2)
                    unit(n, i, ps_y[:, u // 2, :], act_hi, act_lo, k0=h * KH2, first=(h == 0), last=(h == 1))

            def run_ffn(ffn, version, version_out):
                up(ffn, version, 0, True)
                with pe.Fori(1, KF // 2) as i:
                    up(ffn, version, i, False)
                with pe.Fori(0, KD // 2) as i:
                    down(ffn, version_out, i)

            pe.wait_ge(const_landed, 16)
            pe.wait_ge(rows_landed, 16 * 9)
            nc.tensor.transpose(ps_aux[:, 0:N_ROWS], rows[:, :], ident[0:N_ROWS, 0:N_ROWS]).then_inc(aux_done, 1)
            for q in range(NQ):
                pe.wait_ge(x_landed[q], 16)
            for d in range(KD):
                at_least(pe, x_ready, d - 1)
                for q in range(NQ):
                    turned = nc.tensor.transpose(ps_y[:, d % 2, q * P:(q + 1) * P], x_in[:, q, d * P:(d + 1) * P], ident)
                turned.then_inc(x_turned, 1)
            pe.wait_ge(aux_free, 1)
            pe.wait_ge(pos_ready, 1)
            mm(ps_aux[:, :], ones[0:1, :], pos_f[0:1, :], start=True, stop=True).then_inc(aux_done, 1)

            run_ffn(0, 0, 1)

            def project(n, i, p, **kw):
                at_least(pe, proj_scaled, p - 3 + 4 * i)
                unit(n, i, ps_s[:, p % 4, :], xg_hi, xg_lo, **kw)

            def aux_start(name, i=0):
                pe.wait_ge(aux_free, AUX.index(name) + i)

            def head_stat(name, tile, i=0):
                pe.wait_ge(head_sq, head_tiles(name) + i)
                pe.wait_ge(ms_ready, STATS.index(name) + i)
                mm(ps_stat[:, :], block_ones, tile, start=True, stop=True).then_inc(stat_done, 1)

            def rotate(name, slot_, i=0):
                aux_start("rot_" + name, i)
                pe.wait_ge(gained, head_tiles(name) + i)
                mm(ps_aux[:, :], rot, work[:, slot_, :], start=True, stop=True).then_inc(aux_done, 1)

            def turn_vt(name, count, rows_):
                aux_start(name)
                pe.wait_ge(proj_scaled, count)
                for q in range(NQ):
                    t = nc.tensor.transpose(ps_aux[:, q * rows_:(q + 1) * rows_], vt[0:rows_, q * P:(q + 1) * P],
                                            ident[0:rows_, 0:rows_])
                t.then_inc(aux_done, 1)

            def compress(c):
                p = 7 + c
                pe.wait_ge(proj_scaled, p - 3)
                pe.wait_ge(blk_lo_ready, c + 1)
                for h in range(2):
                    n = U_W1 + 2 * c + h
                    pe.wait_ge(lo_ready, n + 1)
                    for k in range(KD):
                        at = (h * KD + k) * 2 * NCP
                        b_hi, b_lo = pt_b[:, c, at:at + 2 * NCP], pt_b[:, c, 2 * T + at:2 * T + at + 2 * NCP]
                        last_mm = three(ps_s[:, p % 4, 0:2 * NCP],
                                        w_hi[:, n % 2, k * P:(k + 1) * P], w_lo[:, n % 2, k * P:(k + 1) * P],
                                        b_hi, b_lo, h == 0 and k == 0, h == 1 and k == KD - 1)
                    last_mm.then_inc(unit_done, 1)

            project(U_MIX, 0, 0, version=1)
            pe.wait_ge(ss_step, KD * 2)
            stat(STATS.index("x1"), ones, ss[:, :])
            project(U_MIX + 1, 0, 1)
            project(U_MIX + 2, 0, 2)
            head_stat("ks", sq[:, :])
            project(U_MIX + 3, 0, 3)
            head_stat("kw", sq[:, :])
            rotate("ks", 0)
            project(U_MIX + 4, 0, 4)
            rotate("kw", 1)
            project(U_MIX + 5, 0, 5)
            turn_vt("t_vs", 5, P)
            project(U_MIX + 6, 0, 6)
            turn_vt("t_vw", 6, P)
            compress(0)
            turn_vt("t_gates", 7, 24)
            compress(1)

            def project_four(b, i, extra=None):
                for u in range(4):
                    project(U_LOOP + 4 * b + u, i, 9 + 4 * b + u)
                    if u == 0 and extra:
                        extra[0]()
                    if u == 1:
                        head_stat("q3" if b else "q0", sq[:, :], i)
                        if extra:
                            extra[1]()
                    if u == 2:
                        if extra:
                            extra[2]()
                        rotate("q3" if b else "q0", 0, i)

            with pe.Fori(0, 3) as i:
                project_four(0, i)

            aux_start("w2")
            pe.wait_ge(w2_lo_ready, 1)
            for c in range(2):
                pe.wait_ge(hid_lo_ready, c + 1)
                last_mm = three(ps_aux[:, c * 2 * NCP:(c + 1) * 2 * NCP], w2_hi[:, c, :], w2_lo[:, c, :],
                                hid_hi[:, c, :], hid_lo[:, c, :], True, True)
            last_mm.then_inc(aux_done, 1)

            def kc_stat():
                pe.wait_ge(head_sq, head_tiles("kc"))
                pe.wait_ge(ms_ready, STATS.index("kc"))
                mm(ps_stat[:, 0:2 * NCP], block_ones, kcm[:, 0, :], start=True, stop=True).then_inc(stat_done, 1)

            def kc_rotate():
                aux_start("rot_kc")
                pe.wait_ge(gained, head_tiles("kc"))
                mm(ps_aux[:, 0:2 * NCP], rot, kcv[:, 0, :], start=True, stop=True).then_inc(aux_done, 1)

            def vc_turn():
                aux_start("t_vc")
                for g in range(2):
                    t = nc.tensor.transpose(ps_aux[0:NCP, g * DH:(g + 1) * DH], kcv[0:DH, 1, g * NCP:(g + 1) * NCP],
                                            ident[0:DH, 0:DH])
                t.then_inc(aux_done, 1)

            project_four(3, 0, (kc_stat, kc_rotate, vc_turn))

            def scores(j, s):
                j, s = j + s // 8, s % 8
                g, c = s // 4, s % 4
                width = (c + 1) * P
                pe.wait_ge(qp_lo_ready, 2 * j + g + 1)
                at_least(pe, exp_done, 8 * j + s - 1)
                query = q_parts[:, g, c * P:(c + 1) * P]
                for br in range(2):
                    bank = ps_s[:, 2 * (s % 2) + br, :]
                    mm(bank[:, 0:width], query, k_hi[:, br, g, 0:width], start=True, stop=False)
                    mm(bank[:, c * P:width], ident_b[:, :], mask_b[:, 0:P], start=False, stop=False)
                    last_mm = mm(bank[:, 0:width], query, k_lo[:, br, g, 0:width], start=False, stop=True)
                last_mm.then_inc(qk_done, 1)

            def scores_c(j, g):
                pe.wait_ge(qp_lo_ready, 2 * j + g + 1)
                if g or not isinstance(j, int):
                    pe.wait_ge(c_pt_lo_ready, 2 * j + g)
                for c in range(NQ):
                    bank = ps_stat[:, c * NCP:(c + 1) * NCP]
                    query = q_parts[:, g, c * P:(c + 1) * P]
                    mm(bank, query, kc_hi[:, g, :], start=True, stop=False)
                    mm(bank, ident_b[:, :], mask_b[:, P + c * NCP:P + (c + 1) * NCP], start=False, stop=False)
                    last_mm = mm(bank, query, kc_lo[:, g, :], start=False, stop=True)
                last_mm.then_inc(c_qk_done, 1)

            def turn_c(j, g):
                pe.wait_ge(c_p_scaled, 2 * j + g + 1)
                for c in range(NQ):
                    t = nc.tensor.transpose(ps_stat[0:NCP, c * P:(c + 1) * P], prob_c[:, c, :], ident)
                t.then_inc(c_pt_done, 1)

            def turn(j, s):
                c = s % 4
                pe.wait_ge(scale_ready, 8 * j + s + 1)
                at_least(pe, pt_lo_ready, 8 * j + s)
                for br in range(2):
                    for k in range(c + 1):
                        at = br * T + k * P
                        t = mm(ps_y[:, br, k * P:(k + 1) * P], prob_of(s)[:, at:at + P], diagonal(s, br),
                               start=True, stop=True)
                t.then_inc(pt_done, 1)

            def values(j, pair):
                j, pair = j + pair // 4, pair % 4
                pe.wait_ge(pt_lo_ready, 8 * j + 2 * pair + 2)
                bank = ps_aux[:, (pair % 2) * 2 * P:(pair % 2 + 1) * 2 * P]
                half_pair = pair % 2
                p_hi, p_lo = turned_parts(pair % 2)
                queries = slice(pair % 2 * 2 * P, (pair % 2 + 1) * 2 * P)
                pe.wait_ge(c_pt_lo_ready, 2 * j + pair // 2 + 1)
                three(bank, vc_hi[:, :], vc_lo[:, :], ptc[:, 0, queries], ptc[:, 1, queries], True, False)
                for br in range(2):
                    for k in reversed(range(2 * half_pair + 2)):
                        skip = P if k == 2 * half_pair + 1 else 0
                        at = (br * 4 + k) * 2 * P + skip
                        last_mm = three(bank[:, skip:], v_hi[:, br, k * P:(k + 1) * P], v_lo[:, br, k * P:(k + 1) * P],
                                        p_hi[:, at:at + 2 * P - skip], p_lo[:, at:at + 2 * P - skip],
                                        False, br == 1 and k == 0)
                last_mm.then_inc(pv_done, 1)

            def attend(j, first=False, last=False):
                for s in range(8):
                    if not (last and s + 2 >= 8):
                        scores(j, s + 2)
                    if s % 2 and not (first and s == 1):
                        values(j, (s - 3) // 2)
                    if s in (2, 6):
                        turn_c(j, s // 4)
                    turn(j, s)
                    if s in (3, 7) and not (last and s == 7):
                        scores_c(j + s // 7, 1 - s // 7)

            pe.wait_ge(proj_scaled, 25)
            pe.wait_ge(aux_free, len(AUX))
            pe.wait_ge(ms_ready, STATS.index("q3") + 1)
            pe.wait_ge(kc_ready, 1)
            pe.wait_ge(k_lo_ready, 2)
            pe.wait_ge(consts_cast, 2)
            scores(0, 0)
            scores_c(0, 0)
            scores(0, 1)
            attend(0, first=True)
            with pe.Fori(1, 3) as j:
                attend(j)
            attend(3, last=True)
            values(3, 3)

            for d in range(KD):
                n = U_OUT + d
                pe.wait_ge(x_ready, KD * 2 + d - 1)
                pe.wait_ge(lo_ready, n + 1)
                for k in range(4, KD):
                    three(ps_y[:, d % 2, :], w_hi[:, n % 2, k * P:(k + 1) * P], w_lo[:, n % 2, k * P:(k + 1) * P],
                          tile_of(ob_hi, k - 4), tile_of(ob_lo, k - 4), k == 4, False)
                if d == 0:
                    pe.wait_ge(o_lo_ready, 16)
                for k in range(4):
                    last_mm = three(ps_y[:, d % 2, :], w_hi[:, n % 2, k * P:(k + 1) * P],
                                    w_lo[:, n % 2, k * P:(k + 1) * P],
                                    tile_of(xg_hi, k), tile_of(xg_lo, k), False, k == 3)
                last_mm.then_inc(unit_done, 1)

            run_ffn(1, 2, 3)
            run_ffn(2, 3, 4)

            pe.wait_ge(ss_step, KD * 5)
            stat(STATS.index("x4"), ones, ss[:, :])
            for g in range(4):
                n = U_POOL + g
                pe.wait_ge(lo_ready, n + 1)
                pe.wait_ge(diff_lo_ready, g + 1)
                for o in range(2):
                    pe.wait_ge(x_ready, KD * 5 + 2 * g + o - 1)
                    for k in range(2):
                        at = (2 * k + o) * P
                        last_mm = three(ps_y[:, o, :], w_hi[:, n % 2, at:at + P], w_lo[:, n % 2, at:at + P],
                                        tile_of(xg_hi, 2 * g + k), tile_of(xg_lo, 2 * g + k), k == 0, k == 1)
                last_mm.then_inc(unit_done, 1)

            run_ffn(3, 5, 6)
            for d in range(KD):
                pe.wait_ge(x_ready, KD * 6 + d + 1)
                at_least(pe, out_copied, d - 1)
                for q in range(NQ):
                    t = nc.tensor.transpose(ps_s[:, d % 2, q * P:(q + 1) * P], x_t[:, d * T + q * P:d * T + (q + 1) * P],
                                            ident)
                t.then_inc(out_turned, 1)

        @block.scalar
        def _(act):
            def copy(dst, src):
                return nc.scalar.copy(dst, src)

            def split(n, i=0):
                at_least(act, unit_done, n - 1 + 4 * i)
                act.wait_ge(raw_landed[n % 4], landed_by(n) + 16 * DMAS[n] * i)
                copy(w_hi[:, n % 2, 0:BLOCKS[n] * P], raw[:, n % 4, 0:BLOCKS[n] * P]).then_inc(hi_ready, 1)

            def pool_x(g):
                for o in range(2):
                    take_x(5, 2 * g + o, R_FFN + 24)

            def xg_high(d, gain):
                nc.scalar.activation(tile_of(xg_hi, d), tile_of(x_t, d), ACT.Copy,
                                     scale=cols[:, bass.ds(gain + d, 1)]).then_inc(xg_hi_ready, 1)

            def take_x(version, d, gain):
                at_least(act, ss_step, KD * version + d)
                act.wait_ge(x_ready, KD * version + d + 1)
                if gain is not None:
                    xg_high(d, gain)
                nc.scalar.activation(sq[:, :], tile_of(x_t, d), ACT.Square).then_inc(sq_ready, 1)

            def root(name, width, cols_=T, i=0):
                index = STATS.index(name) + i
                act.wait_ge(stat_done, index + 1)
                at_least(act, root_ready, index)
                nc.scalar.activation(ms[:, 0:cols_], ps_stat[:, 0:cols_], ACT.Sqrt, scale=1.0 / width,
                                     bias=eps_col[:, :]).then_inc(ms_ready, 1)

            def up(ffn, b, i):
                for u in range(4):
                    f = 2 * (b + i) + u // 2
                    split(U_FFN[ffn] + 4 * b + u + 2, i)
                    if u % 2 == 0:
                        act.wait_ge(gate_scaled, KF * ffn + f + 1)
                        nc.scalar.activation(work[:, u // 2, :], work[:, u // 2, :], ACT.Silu).then_inc(silu_ready, 1)
                    else:
                        act.wait_ge(a_ready, KF * ffn + f + 1)
                        copy(tile_of(act_hi, f), work[:, u // 2, :]).then_inc(act_hi_ready, 1)

            def down(ffn, version_out, gain, b, i, last=False):
                for u in range(4):
                    d = 2 * (b + i) + u // 2
                    n = U_FFN[ffn] + 2 * KF + 4 * b + u + 2
                    if n < U_END:
                        split(n, i)
                    if u % 2 and version_out < 6:
                        take_x(version_out, d, gain)

            def run_ffn(ffn, version, version_out, gain):
                root(f"x{version}", D)
                nc.scalar.preload_act_table(ACT.Silu)
                with act.Fori(0, KF // 2 - 1) as i:
                    up(ffn, 0, i)
                up(ffn, KF // 2 - 1, 0)
                if ffn == 0:
                    rope_tables()
                with act.Fori(0, KD // 2 - 1) as i:
                    down(ffn, version_out, gain, 0, i)
                down(ffn, version_out, gain, KD // 2 - 1, 0)

            def rope_tables():
                act.wait_ge(turn_ready, 1)
                nc.scalar.activation(turns, ang, ACT.Abs).then_inc(trig_ready, 1)
                nc.scalar.activation(sin_t[:, 0:T], ang, ACT.Sin).then_inc(trig_ready, 1)
                act.wait_ge(trig_ready, 2)
                nc.scalar.activation(cos_t[:, 0:T], turns, ACT.Sin, scale=-1.0,
                                     bias=half[:, :]).then_inc(trig_ready, 1)

            act.dma_start(rows[R_FFN:R_MIX, :], A["ffn_norm"].rearrange("l h (k p) -> (l h k) p", p=P)).then_inc(rows_landed, 16)
            act.dma_start(rows[R_MIX:R_PSC, :], A["mix_norm"].rearrange("l (k p) -> (l k) p", p=P)).then_inc(rows_landed, 16)
            act.dma_start(rows[R_PSC:R_CONV, :], A["pool_scale"].rearrange("l (k p) -> (l k) p", p=P)).then_inc(rows_landed, 16)
            act.dma_start(rows[R_CONV:R_QN, :], A["hyb_conv_w"].rearrange("l i (k p) -> (l i k) p", p=P)).then_inc(rows_landed, 16)
            for g in range(2):
                act.dma_start(rows[R_QN:R_KN, g * DH:(g + 1) * DH], A["hyb_q_norm"]).then_inc(rows_landed, 16)
                act.dma_start(rows[R_KN:R_POS, g * DH:(g + 1) * DH], A["hyb_k_norm"][0]).then_inc(rows_landed, 16)
            act.dma_start(rows[R_POS:N_ROWS, :], A["hyb_cmp_pos"].rearrange("l c (j e) d -> (l c j) (e d)", e=2)).then_inc(rows_landed, 16)
            act.dma_start(consts[:, :], A["consts"]).then_inc(const_landed, 16)
            act.dma_start(pos_i[:, :], A["positions"]).then_inc(pos_landed, 16)
            for g in range(2):
                act.dma_start(w2_raw[:, :, g, :], A["hyb_cmp_w2"][0].rearrange("c h d -> h c d")).then_inc(w2_landed, 16)
            act.wait_ge(const_landed, 16)
            copy(ident_b[:, :], ident).then_inc(consts_cast, 1)
            copy(mask_b[:, :], consts[:, C_MASK:C_CMASK + NQ * NCP]).then_inc(consts_cast, 1)
            act.wait_ge(aux_free, 1)
            for d in range(KD):
                take_x(0, d, R_FFN)
            split(0)
            split(1)
            run_ffn(0, 0, 1, R_MIX)

            def square(name, dst, src, i=0):
                act.wait_ge(stat_done, STATS.index(name) + i)
                nc.scalar.activation(dst, src, ACT.Square).then_inc(head_sq, 1)

            def split_keys(br):
                act.wait_ge(rope_ready, head_tiles("ks") + br)
                for g in range(2):
                    for h in range(2):
                        last = copy(k_hi[h * DH:(h + 1) * DH, br, g, :], work[g * DH:(g + 1) * DH, br, :])
                last.then_inc(k_hi_ready, 1)

            def split_values(br):
                act.wait_ge(aux_done, AUX.index("t_vs") + br + 1)
                copy(v_hi[:, br, :], ps_aux[:, :]).then_inc(v_hi_ready, 1)

            def split_blocks(c):
                act.wait_ge(blk_step, 4 * (c + 1))
                copy(pt_b[:, c, 0:2 * T], qf[:, c * 2 * T:(c + 1) * 2 * T]).then_inc(blk_hi_ready, 1)

            def tanh(c):
                act.wait_ge(gelu_in, c + 1)
                nc.scalar.activation(hid[:, 1, c, :], hid[:, 1, c, :], ACT.Tanh, scale=0.7978845608028654).then_inc(gelu_tanh, 1)

            def split_hidden(c):
                act.wait_ge(hid_ready, c + 1)
                copy(hid_hi[:, c, :], hid[:, 0, c, :]).then_inc(hid_hi_ready, 1)

            def kc_square():
                square_in = kcv[:, 0, :]
                act.wait_ge(aux_free, AUX.index("w2") + 1)
                nc.scalar.activation(kcm[:, 0, :], square_in, ACT.Square).then_inc(head_sq, 1)

            def kc_split():
                act.wait_ge(rope_ready, head_tiles("kc"))
                for g in range(2):
                    last = copy(kc_hi[:, g, :], kcv[:, 0, g * NCP:(g + 1) * NCP])
                last.then_inc(kc_hi_ready, 1)
                act.wait_ge(aux_done, AUX.index("t_vc") + 1)
                copy(vc_hi[:, :], ps_aux[0:NCP, 0:P]).then_inc(v_hi_ready, 1)

            split(U_MIX + 2)
            root("x1", D)
            act.wait_ge(proj_scaled, 1)
            square("ks", sq[:, :], work[:, 0, :])
            split(U_MIX + 3)
            split(U_MIX + 4)
            root("ks", DH)
            act.wait_ge(proj_scaled, 2)
            square("kw", sq[:, :], work[:, 1, :])
            act.wait_ge(w2_landed, 32)
            copy(w2_hi[:, :, :], w2_raw[:, :, :, :].rearrange("p c g d -> p c (g d)")).then_inc(w2_hi_ready, 1)
            split(U_MIX + 5)
            root("kw", DH)
            split(U_MIX + 6)
            split_keys(0)
            split(U_W1)
            split_keys(1)
            split_blocks(0)
            split(U_W1 + 1)
            split_values(0)
            split_blocks(1)
            split(U_W1 + 2)
            split_values(1)
            split(U_W1 + 3)
            act.wait_ge(aux_done, AUX.index("t_gates") + 1)
            nc.scalar.activation(gate[:, 0, :], ps_aux[:, 0:NQ * 24], ACT.Exp, scale=-1.0).then_inc(gate_exp, 1)
            tanh(0)
            split_hidden(0)
            split(U_LOOP)
            split(U_LOOP + 1)
            tanh(1)
            split_hidden(1)

            def project_four(b, i):
                for u in range(4):
                    n = U_LOOP + 4 * b + u
                    split(n + 2, i)
                    if u == 0:
                        if b:
                            root("kc", DH, 2 * NCP)
                        act.wait_ge(proj_scaled, 10 + 4 * b + 4 * i)
                        square("q3" if b else "q0", sq[:, :], work[:, 0, :], i)
                    if u == 1:
                        root("q3" if b else "q0", DH, i=i)
                    if u == 2 and b:
                        kc_split()
                    if u == 3:
                        act.wait_ge(ob_ready, b + i + 1)
                        copy(tile_of(ob_hi, b + i), work2[:, :]).then_inc(ob_hi_ready, 1)

            with act.Fori(0, 3) as i:
                project_four(0, i)
            kc_square()
            project_four(3, 0)

            def split_query(j, g):
                act.wait_ge(rope_ready, head_tiles("q3"))
                at_least(act, qk_done, 8 * j - 4 + 4 * g)
                rows_ = slice(g * DH, (g + 1) * DH)
                copy(q_parts[rows_, g, :], qf[rows_, bass.ds(j * T, T)]).then_inc(qp_hi_ready, 1)

            def exps(j, s):
                j, s = j + s // 8, s % 8
                c = s % 4
                width = (c + 1) * P
                act.wait_ge(negmax_ready, 8 * j + s + 1)
                for br in range(2):
                    last = nc.scalar.activation(prob_of(s)[:, br * T:br * T + width], ps_s[:, 2 * (s % 2) + br, 0:width],
                                                ACT.Exp, bias=small[:, s % 2, br:br + 1], scale=DH ** -0.5,
                                                accum_out=small[:, s % 2, 2 + br:3 + br])
                last.then_inc(exp_done, 1)

            def exps_c(j, g):
                act.wait_ge(c_negmax_ready, 2 * j + g + 1)
                for c in range(NQ):
                    last = nc.scalar.activation(prob_c[:, c, :], ps_stat[:, c * NCP:(c + 1) * NCP], ACT.Exp,
                                                bias=small_c[:, 0, c:c + 1], scale=DH ** -0.5,
                                                accum_out=small_c[:, 1, c:c + 1])
                last.then_inc(c_exp_done, 1)

            def split_c(j, g):
                act.wait_ge(c_pt_done, 2 * j + g + 1)
                copy(ptc[:, 0, :], ps_stat[0:NCP, :]).then_inc(c_pt_hi_ready, 1)

            def split_probs(j, s):
                j, s = j + s // 8, s % 8
                c = s % 4
                pair = s // 2
                act.wait_ge(pt_done, 8 * j + s + 1)
                p_hi = turned_parts(pair % 2)[0].rearrange("p (b k h q) -> p b k h q", b=2, k=4, h=2)
                copy(p_hi[:, :, 0:c + 1, c % 2, :],
                     ps_y[:, :, 0:(c + 1) * P].rearrange("p b (k q) -> p b k q", q=P)).then_inc(pt_hi_ready, 1)

            def split_output(j, pair):
                j, pair = j + pair // 4, pair % 4
                act.wait_ge(pv_done, 4 * j + pair + 1)
                g, c = pair // 2, pair % 2
                rows_ = slice(g * DH, (g + 1) * DH)
                copy(xg_hi[rows_, bass.ds(j * T + c * 2 * P, 2 * P)],
                     ps_aux[rows_, c * 2 * P:(c + 1) * 2 * P]).then_inc(o_hi_ready, 1)

            def attend(j, first=False, last=False):
                for s in range(8):
                    if s % 2 == 0 and not (first and s <= 2):
                        split_output(j, (s - 4) // 2)
                    if not (first and s == 0):
                        split_probs(j, s - 1)
                    if not (last and s == 7):
                        exps(j, s + 1)
                    if s in (2, 6):
                        split_c(j, s // 4)
                    if s in (0, 4) and not (first and s == 0):
                        exps_c(j, s // 4)
                    if s in (3, 7) and not last:
                        split_query(j + 1, s // 4)

            split_query(0, 0)
            split_query(0, 1)
            exps(0, 0)
            exps_c(0, 0)
            attend(0, first=True)
            with act.Fori(1, 3) as j:
                attend(j)
            attend(3, last=True)
            split_output(3, 2)
            split_probs(3, 7)
            split_output(3, 3)

            for d in range(KD):
                split(U_OUT + d + 2)
                take_x(2, d, R_FFN + 8 if d >= LATE else None)
            act.wait_ge(unit_done, U_OUT + KD)
            for d in range(LATE):
                xg_high(d, R_FFN + 8)
            run_ffn(1, 2, 3, R_FFN + 16)
            run_ffn(2, 3, 4, None)

            root("x4", D)
            for g in range(4):
                act.wait_ge(diff_ready, g + 1)
                copy(xg_hi[:, 2 * g * T:(2 * g + 2) * T], diff[:, g % 2, :]).then_inc(diff_hi_ready, 1)
                if g:
                    split(U_POOL + g + 1)
                    pool_x(g - 1)
            split(U_POOL + 5)
            pool_x(3)
            run_ffn(3, 5, 6, None)

        @block.vector
        def _(dve):
            tt = nc.vector.tensor_tensor
            stt = nc.vector.scalar_tensor_tensor
            ts = nc.vector.tensor_scalar
            steps = [0]

            def then(ins):
                steps[0] += 1
                ins.then_inc(dve_step, 1)
                dve.wait_ge(dve_step, steps[0])

            def split(n, i=0):
                dve.wait_ge(hi_ready, n + 1 + 4 * i)
                size = BLOCKS[n] * P
                tt(w_lo[:, n % 2, 0:size], raw[:, n % 4, 0:size], f32(w_hi[:, n % 2, 0:size]),
                   ALU.subtract).then_inc(lo_ready, 1)

            def invert(name, dst, cols_=T, i=0):
                if name[0] != "x":
                    at_least(dve, gained, head_tiles(name) - 1 + i)
                dve.wait_ge(ms_ready, STATS.index(name) + i + 1)
                nc.vector.reciprocal(dst, ms[:, 0:cols_]).then_inc(root_ready, 1)

            def xg_low(version, d, gain):
                place = (d - LATE) % KD if version == 2 else d
                dve.wait_ge(xg_hi_ready, KD * XG_OF[version] + place + 1)
                stt(tile_of(xg_lo, d), tile_of(x_t, d), cols[:, bass.ds(gain + d, 1)], f32(tile_of(xg_hi, d)),
                    ALU.mult, ALU.subtract).then_inc(xg_lo_ready, 1)

            def up(ffn, version, b, i):
                for u in range(4):
                    n, f = U_FFN[ffn] + 4 * b + u, 2 * (b + i) + u // 2
                    split(n + 2, i)
                    dve.wait_ge(unit_done, n + 1 + 4 * i)
                    dve.wait_ge(root_ready, STATS.index(f"x{version}") + 1)
                    if u % 2 == 0:
                        tt(work[:, u // 2, :], ps_s[:, u // 2, :], rstd[:, :], ALU.mult).then_inc(gate_scaled, 1)
                    else:
                        a = work[:, u // 2, :]
                        tt(work2[:, :], ps_s[:, 2 + u // 2, :], rstd[:, :], ALU.mult).then_inc(up_scaled, 1)
                        dve.wait_ge(silu_ready, KF * ffn + f + 1)
                        dve.wait_ge(up_scaled, KF * ffn + f + 1)
                        tt(a, a, work2[:, :], ALU.mult).then_inc(a_ready, 1)
                        dve.wait_ge(act_hi_ready, KF * ffn + f + 1)
                        tt(tile_of(act_lo, f), a, f32(tile_of(act_hi, f)), ALU.subtract).then_inc(act_lo_ready, 1)

            def down(ffn, version_out, gain, b, i):
                for u in range(4):
                    n, d = U_FFN[ffn] + 2 * KF + 4 * b + u, 2 * (b + i) + u // 2
                    if n + 2 < U_END:
                        split(n + 2, i)
                    if u % 2:
                        dve.wait_ge(unit_done, n + 1 + 4 * i)
                        stt(tile_of(x_t, d), ps_y[:, u // 2, :], 0.5, tile_of(x_t, d), ALU.mult,
                            ALU.add).then_inc(x_ready, 1)
                        if gain is not None:
                            xg_low(version_out, d, gain)

            def run_ffn(ffn, version, version_out, gain):
                invert(f"x{version}", rstd[:, :])
                with dve.Fori(0, KF // 2 - 1) as i:
                    up(ffn, version, 0, i)
                up(ffn, version, KF // 2 - 1, 0)
                with dve.Fori(0, KD // 2 - 1) as i:
                    down(ffn, version_out, gain, 0, i)
                down(ffn, version_out, gain, KD // 2 - 1, 0)

            nc.vector.memset(eps_col[:, :], EPS)
            then(nc.vector.memset(half[:, :], float(np.pi / 2)))
            dve.wait_ge(aux_done, 1)
            nc.vector.tensor_copy(cols[:, :], ps_aux[:, 0:N_ROWS]).then_inc(aux_free, 1)
            dve.wait_ge(pos_landed, 16)
            nc.vector.tensor_copy(pos_f[:, :], pos_i[:, :]).then_inc(pos_ready, 1)
            for d in range(KD):
                dve.wait_ge(x_turned, d + 1)
                nc.vector.tensor_copy(tile_of(x_t, d), ps_y[:, d % 2, :]).then_inc(x_ready, 1)
                if d:
                    xg_low(0, d - 1, R_FFN)
            xg_low(0, KD - 1, R_FFN)
            split(0)
            split(1)
            dve.wait_ge(aux_done, 2)
            ts(ang, ps_aux[:, :], freq, None, ALU.mult).then_inc(aux_free, 1)
            run_ffn(0, 0, 1, R_MIX)

            def scaled(n, p, dst, src_rows=slice(0, P), i=0):
                dve.wait_ge(unit_done, n + 1 + 4 * i)
                tt(dst, ps_s[src_rows, p % 4, :], rstd[src_rows, :], ALU.mult).then_inc(proj_scaled, 1)

            def gain_and_norm(name, gain, dst, cols_=T, i=0):
                dve.wait_ge(root_ready, STATS.index(name) + 1 + i)
                stt(dst, dst, cols[:, gain:gain + 1], ss[:, 0:cols_], ALU.mult, ALU.mult).then_inc(gained, 1)

            def rope(name, dst, i=0):
                dve.wait_ge(aux_done, AUX.index("rot_" + name) + 1 + i)
                dve.wait_ge(m1_ready, head_tiles(name) + i)
                tt(dst, ps_aux[:, :], sin_t[:, 0:T], ALU.mult).then_inc(aux_free, 1)
                dve.wait_ge(aux_free, AUX.index("rot_" + name) + 1 + i)
                tt(dst, dst, m1[:, :], ALU.add).then_inc(rope_ready, 1)

            def keys_low(br):
                dve.wait_ge(k_hi_ready, br + 1)
                for g in range(2):
                    rows_ = slice(g * DH, (g + 1) * DH)
                    for h in range(2):
                        last = tt(k_lo[h * DH:(h + 1) * DH, br, g, :], work[rows_, br, :], f32(k_hi[rows_, br, g, :]),
                                  ALU.subtract)
                last.then_inc(k_lo_ready, 1)

            def values_low(br):
                dve.wait_ge(v_hi_ready, br + 1)
                tt(v_lo[:, br, :], ps_aux[:, :], f32(v_hi[:, br, :]), ALU.subtract).then_inc(aux_free, 1)

            def pairs_of(n, p, c):
                dve.wait_ge(unit_done, n + 1)
                e = prob[:, c, :].rearrange("p (g t) -> p g t", g=2)
                for g in range(2):
                    rows_ = slice(g * DH, (g + 1) * DH)
                    tt(e[0:DH, g, 0:T], ps_s[rows_, p % 4, :], rstd[rows_, :], ALU.mult).then_inc(pair_step, 1)
                    last = tt(e[DH:P, g, 0:T - 1], ps_s[rows_, p % 4, 1:T], rstd[rows_, 1:T], ALU.mult)
                    if g == 0:
                        last.then_inc(pair_step, 1)
                last.then_inc(proj_scaled, 1)

            def blocks(c):
                dve.wait_ge(pair_step, 3 * (c + 1))
                dve.wait_ge(proj_scaled, 3 + c)
                e = prob[:, c, :].rearrange("p (g m b e) -> p g b m e", g=2, b=8, e=2)
                dst = qf[:, c * 2 * T:(c + 1) * 2 * T].rearrange("p (j g n) -> p g j n", g=2, n=NCP)
                for g in range(2):
                    for a in range(2):
                        at = R_POS + 16 * c + 8 * a
                        tt(dst[:, g, 8 * a:8 * a + 8, :], e[:, g, :, a:a + NCP, 0],
                           cols[:, at:at + 8].unsqueeze(2).to_broadcast([P, 8, NCP]), ALU.add).then_inc(blk_step, 1)

            def blocks_low(c):
                dve.wait_ge(blk_hi_ready, c + 1)
                tt(pt_b[:, c, 2 * T:4 * T], qf[:, c * 2 * T:(c + 1) * 2 * T], f32(pt_b[:, c, 0:2 * T]),
                   ALU.subtract).then_inc(blk_lo_ready, 1)

            def gelu_argument(c):
                n, p = U_W1 + 2 * c + 1, 7 + c
                x, arg = hid[:, 0, c, :], hid[:, 1, c, :]
                dve.wait_ge(unit_done, n + 1)
                tt(x, ps_s[:, p % 4, 0:2 * NCP], ones[:, 0:2 * NCP], ALU.mult).then_inc(proj_scaled, 1)
                dve.wait_ge(proj_scaled, p + 1)
                then(tt(arg, x, x, ALU.mult))
                then(ts(arg, arg, 0.044715, 1.0, ALU.mult, ALU.add))
                tt(arg, arg, x, ALU.mult).then_inc(gelu_in, 1)

            def gelu_result(c):
                x, arg = hid[:, 0, c, :], hid[:, 1, c, :]
                dve.wait_ge(gelu_tanh, c + 1)
                then(stt(arg, arg, 1.0, x, ALU.add, ALU.mult))
                ts(x, arg, 0.5, None, ALU.mult).then_inc(hid_ready, 1)
                dve.wait_ge(hid_hi_ready, c + 1)
                tt(hid_lo[:, c, :], x, f32(hid_hi[:, c, :]), ALU.subtract).then_inc(hid_lo_ready, 1)

            split(U_MIX + 2)
            invert("x1", rstd[:, :])
            dve.wait_ge(root_ready, STATS.index("x1") + 1)
            scaled(U_MIX, 0, work[:, 0, :])
            split(U_MIX + 3)
            scaled(U_MIX + 1, 1, work[:, 1, :])
            split(U_MIX + 4)
            invert("ks", ss[:, :])
            gain_and_norm("ks", R_KN + 1, work[:, 0, :])
            dve.wait_ge(mix_zeroed, 1)
            pairs_of(U_MIX + 2, 2, 0)
            split(U_MIX + 5)
            invert("kw", ss[:, :])
            gain_and_norm("kw", R_KN + 2, work[:, 1, :])
            pairs_of(U_MIX + 3, 3, 1)
            split(U_MIX + 6)
            rope("ks", work[:, 0, :])
            scaled(U_MIX + 4, 4, vt[:, :])
            blocks(0)
            split(U_W1)
            rope("kw", work[:, 1, :])
            dve.wait_ge(aux_done, AUX.index("t_vs") + 1)
            scaled(U_MIX + 5, 5, vt[:, :])
            blocks_low(0)
            split(U_W1 + 1)
            values_low(0)
            dve.wait_ge(aux_done, AUX.index("t_vw") + 1)
            scaled(U_MIX + 6, 6, vt[:, :])
            blocks(1)
            split(U_W1 + 2)
            values_low(1)
            blocks_low(1)
            keys_low(0)
            split(U_W1 + 3)
            gates_in = gate[:, 1, :]
            dve.wait_ge(gate_exp, 1)
            ts(gates_in, gate[:, 0, :], 1.0, None, ALU.add).then_inc(aux_free, 1)
            dve.wait_ge(aux_free, AUX.index("t_gates") + 1)
            then(nc.vector.reciprocal(gates_in, gates_in))
            cmp_gates = gate[:, 1, 0:24].rearrange("p (h b) -> p h b", b=3)[:, :, 0]
            then(ts(cmp_gates, cmp_gates, consts[:, C_VALID:C_VALID + 1], None, ALU.mult))
            gelu_argument(0)
            gelu_result(0)
            split(U_LOOP)
            keys_low(1)
            split(U_LOOP + 1)
            gelu_argument(1)
            gelu_result(1)
            dve.wait_ge(w2_hi_ready, 1)
            tt(w2_lo[:, :, :], w2_raw[:, :, :, :].rearrange("p c g d -> p c (g d)"), f32(w2_hi[:, :, :]),
               ALU.subtract).then_inc(w2_lo_ready, 1)

            def project_four(b, i, extra=None):
                j = b + i
                name = "q3" if b else "q0"
                v, y = work[:, 1, :], vt[:, :]

                def conv_w(k):
                    return cols[:, bass.ds(R_CONV + 4 * k + j, 1)]

                for u in range(4):
                    n, p = U_LOOP + 4 * b + u, 9 + 4 * b + u
                    split(n + 2, i)
                    if u == 0:
                        scaled(n, p, work[:, 0, :], i=i)
                    if u == 1:
                        scaled(n, p, y, i=i)
                        invert(name, ss[:, :], i=i)
                        gain_and_norm(name, R_QN, work[:, 0, :], i=i)
                    if u == 2:
                        scaled(n, p, work2[:, :], i=i)
                        dve.wait_ge(proj_scaled, p + 1 + 4 * i)
                        tt(v, work2[:, :], y, ALU.mult).then_inc(conv_step, 1)
                        dve.wait_ge(conv_step, 4 * b + 1 + 4 * i)
                        ts(y, v, conv_w(2), None, ALU.mult).then_inc(conv_step, 1)
                        dve.wait_ge(conv_step, 4 * b + 2 + 4 * i)
                        stt(y[:, 1:T], v[:, 0:T - 1], conv_w(1), y[:, 1:T], ALU.mult, ALU.add).then_inc(conv_step, 1)
                        dve.wait_ge(conv_step, 4 * b + 3 + 4 * i)
                        stt(y[:, 2:T], v[:, 0:T - 2], conv_w(0), y[:, 2:T], ALU.mult, ALU.add).then_inc(conv_step, 1)
                    if u == 3:
                        scaled(n, p, work2[:, :], i=i)
                        dve.wait_ge(proj_scaled, p + 1 + 4 * i)
                        dve.wait_ge(conv_step, 4 * b + 4 + 4 * i)
                        tt(work2[:, :], work2[:, :], y, ALU.mult).then_inc(ob_ready, 1)
                        rope(name, tile_of(qf, j), i)
                        dve.wait_ge(ob_hi_ready, j + 1)
                        tt(tile_of(ob_lo, j), work2[:, :], f32(tile_of(ob_hi, j)), ALU.subtract).then_inc(ob_lo_ready, 1)
                    if extra and u in extra:
                        extra[u]()

            with dve.Fori(0, 3) as i:
                project_four(0, i)

            def compressed():
                dve.wait_ge(aux_done, AUX.index("w2") + 1)
                tt(kcv[:, :, :].rearrange("p a b -> p (a b)"), ps_aux[:, 0:4 * NCP], ones[:, :],
                   ALU.mult).then_inc(aux_free, 1)

            def kc_norm():
                invert("kc", ss[:, 0:2 * NCP], 2 * NCP)
                gain_and_norm("kc", R_KN, kcv[:, 0, :], 2 * NCP)

            def kc_rope():
                dve.wait_ge(aux_done, AUX.index("rot_kc") + 1)
                dve.wait_ge(m1_ready, head_tiles("kc"))
                kc = kcv[:, 0, :]
                for g in range(2):
                    part = slice(g * NCP, (g + 1) * NCP)
                    s_at = sin_t[:, :].rearrange("p (n e) -> p n e", e=16)[:, 1:NCP + 1, 15]
                    last = tt(kc[:, part], ps_aux[:, part], s_at, ALU.mult)
                    if g == 0:
                        last.then_inc(dve_step, 1)
                        steps[0] += 1
                last.then_inc(aux_free, 1)
                dve.wait_ge(dve_step, steps[0])
                dve.wait_ge(aux_free, AUX.index("rot_kc") + 1)
                tt(kc, kc, kcm[:, 1, :], ALU.add).then_inc(rope_ready, 1)

            def kc_low():
                dve.wait_ge(kc_hi_ready, 1)
                tt(kc_lo[:, :, :].rearrange("p a b -> p (a b)"), kcv[:, 0, :],
                   f32(kc_hi[:, :, :].rearrange("p a b -> p (a b)")), ALU.subtract).then_inc(kc_ready, 1)
                dve.wait_ge(v_hi_ready, 3)
                tt(vc_lo[:, :], ps_aux[0:NCP, 0:P], f32(vc_hi[:, :]), ALU.subtract).then_inc(aux_free, 1)

            compressed()
            project_four(3, 0, {0: kc_norm, 1: kc_rope, 2: kc_low})

            def query_low(j, g):
                dve.wait_ge(qp_hi_ready, 2 * j + g + 1)
                rows_, other = slice(g * DH, (g + 1) * DH), slice((1 - g) * DH, (2 - g) * DH)
                tt(q_parts[other, g, :], qf[rows_, bass.ds(j * T, T)], f32(q_parts[rows_, g, :]),
                   ALU.subtract).then_inc(qp_lo_ready, 1)

            def maxima(j, s):
                j, s = j + s // 8, s % 8
                width = (s % 4 + 1) * P
                m = small[:, s % 2, :]
                dve.wait_ge(qk_done, 8 * j + s + 1)
                nc.vector.reduce_max(m[:, 8:10], ps_s[:, 2 * (s % 2):2 * (s % 2) + 2, 0:width], AX_X).then_inc(max_step, 1)
                dve.wait_ge(max_step, 8 * j + s + 1)
                ts(m[:, 0:2], m[:, 8:10], -DH ** -0.5, None, ALU.mult).then_inc(negmax_ready, 1)

            def maxima_c(j, g):
                dve.wait_ge(c_qk_done, 2 * j + g + 1)
                nc.vector.reduce_max(small_c[:, 4, :], ps_stat[:, 0:NQ * NCP].rearrange("p (c n) -> p c n", n=NCP),
                                     AX_X).then_inc(c_max_step, 1)
                dve.wait_ge(c_max_step, 2 * j + g + 1)
                ts(small_c[:, 0, :], small_c[:, 4, :], -DH ** -0.5, None, ALU.mult).then_inc(c_negmax_ready, 1)

            def scales_c(j, g):
                dve.wait_ge(c_exp_done, 2 * j + g + 1)
                nc.vector.reciprocal(small_c[:, 2, :], small_c[:, 1, :]).then_inc(c_sum_step, 1)
                dve.wait_ge(c_sum_step, 2 * j + g + 1)
                gates_c = gate[:, 1, :].rearrange("p (c x) -> p c x", c=NQ)[:, :, bass.ds(j * 3 + g * 12, 1)]
                tt(small_c[:, 3, :].unsqueeze(2), small_c[:, 2, :].unsqueeze(2), gates_c, ALU.mult).then_inc(c_scale_ready, 1)

            def probs_c_low(j, g):
                dve.wait_ge(c_pt_hi_ready, 2 * j + g + 1)
                tt(ptc[:, 1, :], ps_stat[0:NCP, :], f32(ptc[:, 0, :]), ALU.subtract).then_inc(c_pt_lo_ready, 1)

            def scales(j, s):
                g, c = s // 4, s % 4
                m = small[:, s % 2, :]
                dve.wait_ge(exp_done, 8 * j + s + 1)
                nc.vector.reciprocal(m[:, 4:6], m[:, 2:4]).then_inc(sum_step, 1)
                dve.wait_ge(sum_step, 8 * j + s + 1)
                for br in range(2):
                    last = ts(diagonal(s, br), ident, m[:, 4 + br:5 + br],
                              gate[:, 1, bass.ds(j * 3 + c * 24 + g * 12 + 1 + br, 1)], ALU.mult, ALU.mult)
                last.then_inc(scale_ready, 1)

            def probs_low(j, s):
                j, s = j + s // 8, s % 8
                c, pair = s % 4, s // 2
                dve.wait_ge(pt_hi_ready, 8 * j + s + 1)
                p_hi, p_lo = (x.rearrange("p (b k h q) -> p b k h q", b=2, k=4, h=2)[:, :, 0:c + 1, c % 2, :]
                              for x in turned_parts(pair % 2))
                tt(p_lo, ps_y[:, :, 0:(c + 1) * P].rearrange("p b (k q) -> p b k q", q=P), f32(p_hi),
                   ALU.subtract).then_inc(pt_lo_ready, 1)

            def output_low(j, pair):
                j, pair = j + pair // 4, pair % 4
                dve.wait_ge(o_hi_ready, 4 * j + pair + 1)
                g, c = pair // 2, pair % 2
                rows_, at = slice(g * DH, (g + 1) * DH), bass.ds(j * T + c * 2 * P, 2 * P)
                tt(xg_lo[rows_, at], ps_aux[rows_, c * 2 * P:(c + 1) * 2 * P], f32(xg_hi[rows_, at]),
                   ALU.subtract).then_inc(o_lo_ready, 1)

            def attend(j, first=False, last=False):
                for s in range(8):
                    if not (last and s == 7):
                        maxima(j, s + 1)
                    scales(j, s)
                    if s % 2 == 0 and not (first and s <= 2):
                        output_low(j, (s - 4) // 2)
                    if not (first and s == 0):
                        probs_low(j, s - 1)
                    if s in (2, 6):
                        probs_c_low(j, s // 4)
                    if s in (0, 4) and not (first and s == 0):
                        maxima_c(j, s // 4)
                    if s in (1, 5) and not (first and s == 1):
                        scales_c(j, s // 4)
                    if s in (3, 7) and not last:
                        query_low(j + 1, s // 4)

            query_low(0, 0)
            query_low(0, 1)
            maxima(0, 0)
            maxima_c(0, 0)
            scales_c(0, 0)
            attend(0, first=True)
            with dve.Fori(1, 3) as j:
                attend(j)
            attend(3, last=True)
            output_low(3, 2)
            probs_low(3, 7)
            output_low(3, 3)

            for d in range(KD):
                split(U_OUT + d + 2)
                dve.wait_ge(unit_done, U_OUT + d + 1)
                tt(tile_of(x_t, d), ps_y[:, d % 2, :], tile_of(x_t, d), ALU.add).then_inc(x_ready, 1)
                if d >= LATE:
                    xg_low(2, d, R_FFN + 8)
            for d in range(LATE):
                xg_low(2, d, R_FFN + 8)
            run_ffn(1, 2, 3, R_FFN + 16)
            run_ffn(2, 3, 4, None)

            def pool_input(g):
                for k in range(2):
                    d = 2 * g + k
                    last = stt(h_pad[:, d, 16:TE], tile_of(x_t, d), cols[:, R_MIX + KD + d:R_MIX + KD + d + 1], rstd[:, :],
                               ALU.mult, ALU.mult)
                then(last)
                h = h_pad[:, 2 * g:2 * g + 2, :]
                src, bufs = h, [sum_a, sum_b]
                for level in range(g + 1):
                    dst = bufs[level % 2]
                    back = 1 << level
                    then(tt(dst[:, :, 16:TE], src[:, :, 16:TE], src[:, :, 16 - back:TE - back], ALU.add))
                    src = dst
                then(tt(src[:, :, 16:32], src[:, :, 16:32],
                        consts[:, C_POOL + 16 * g:C_POOL + 16 * g + 16].unsqueeze(1).to_broadcast([P, 2, 16]), ALU.mult))
                if g >= 2:
                    dve.wait_ge(diff_hi_ready, g - 1)
                stt(diff[:, g % 2, :].rearrange("p (k t) -> p k t", k=2), src[:, :, 16:TE], 1.0 / (2 << g), h[:, :, 16:TE],
                    ALU.mult, ALU.subtract).then_inc(diff_ready, 1)

            def pool_x(g):
                dve.wait_ge(unit_done, U_POOL + g + 1)
                for o in range(2):
                    d = 2 * g + o
                    stt(tile_of(x_t, d), ps_y[:, o, :], cols[:, R_PSC + d:R_PSC + d + 1], tile_of(x_t, d), ALU.mult,
                        ALU.add).then_inc(x_ready, 1)
                    xg_low(5, d, R_FFN + 24)

            invert("x4", rstd[:, :])
            dve.wait_ge(root_ready, STATS.index("x4") + 1)
            dve.wait_ge(pool_zeroed, 1)
            for g in range(4):
                pool_input(g)
                dve.wait_ge(diff_hi_ready, g + 1)
                tt(xg_lo[:, 2 * g * T:(2 * g + 2) * T], diff[:, g % 2, :], f32(xg_hi[:, 2 * g * T:(2 * g + 2) * T]),
                   ALU.subtract).then_inc(diff_lo_ready, 1)
                if g:
                    split(U_POOL + g + 1)
                    pool_x(g - 1)
            split(U_POOL + 5)
            pool_x(3)
            run_ffn(3, 5, 6, None)

            for d in range(KD):
                dve.wait_ge(out_turned, d + 1)
                if d >= 2:
                    dve.wait_ge(out_stored[d % 2], 16 * (d // 2))
                nc.vector.tensor_copy(work[:, d % 2, :], ps_s[:, d % 2, :]).then_inc(out_copied, 1)

        @block.gpsimd
        def _(pool):
            tt = nc.gpsimd.tensor_tensor
            ts = nc.gpsimd.tensor_scalar
            steps = [0]

            def then(ins):
                steps[0] += 1
                ins.then_inc(pool_step, 1)
                pool.wait_ge(pool_step, steps[0])

            def sums(version):
                for d in range(KD):
                    pool.wait_ge(sq_ready, KD * version + d + 1)
                    if d == 0:
                        at_least(pool, stat_done, STATS.index(f"x{version}"))
                        nc.gpsimd.tensor_copy(ss[:, :], sq[:, :]).then_inc(ss_step, 1)
                    else:
                        pool.wait_ge(ss_step, KD * version + d)
                        tt(ss[:, :], ss[:, :], sq[:, :], ALU.add).then_inc(ss_step, 1)

            def cosine(name, slot_, i=0):
                pool.wait_ge(gained, head_tiles(name) + i)
                at_least(pool, rope_ready, head_tiles(name) - 1 + i)
                tt(m1[:, :], work[:, slot_, :], cos_t[:, 0:T], ALU.mult).then_inc(m1_ready, 1)

            nc.gpsimd.memset(sin_t[:, T:TE], 0.0)
            then(nc.gpsimd.memset(cos_t[:, T:TE], 0.0))
            sums(0)

            pool.wait_ge(aux_free, 2)
            pool.wait_ge(stat_done, 1)
            for many in (1024.0, 1.0):
                then(ts(turns, ang, 1.0 / (2 * np.pi * many), ROUND, ALU.mult, ALU.add))
                then(ts(turns, turns, ROUND, None, ALU.subtract))
                for part in PI_PARTS:
                    then(ts(step_, turns, part * many, None, ALU.mult))
                    then(tt(ang, ang, step_, ALU.subtract))
            ts(ang, ang, 3.1415925, -3.1415925, ALU.min, ALU.max).then_inc(turn_ready, 1)

            sums(1)
            nc.gpsimd.memset(prob[:, :, :].rearrange("p c (g t) -> p c g t", g=2)[:, :, :, T - 1:TE], 0.0).then_inc(mix_zeroed, 1)
            pool.wait_ge(trig_ready, 3)
            for slot_, name in enumerate(("ks", "kw")):
                cosine(name, slot_)
            with pool.Fori(0, 3) as i:
                cosine("q0", 0, i)
            pool.wait_ge(gained, head_tiles("kc"))
            for g in range(2):
                part = slice(g * NCP, (g + 1) * NCP)
                c_at = cos_t[:, :].rearrange("p (n e) -> p n e", e=16)[:, 1:NCP + 1, 15]
                last = tt(kcm[:, 1, part], kcv[:, 0, part], c_at, ALU.mult)
            last.then_inc(m1_ready, 1)
            cosine("q3", 0)

            with pool.Fori(0, 8) as head:
                pool.wait_ge(c_scale_ready, head + 1)
                tt(prob_c[:, :, :], prob_c[:, :, :], small_c[:, 3, :].unsqueeze(2).to_broadcast([P, NQ, NCP]),
                   ALU.mult).then_inc(c_p_scaled, 1)

            for version in (2, 3, 4):
                sums(version)
            for pad in (h_pad, sum_a, sum_b):
                last = nc.gpsimd.memset(pad[:, :, 0:16], 0.0)
            last.then_inc(pool_zeroed, 1)
            sums(5)


_INS = ["x", "positions", "ffn_norm", "ffn_w_gate", "ffn_w_up", "ffn_w_down", "mix_norm", "hyb_w_in", "hyb_q_norm",
        "hyb_k_norm", "hyb_cmp_pos", "hyb_cmp_w1", "hyb_cmp_w2", "hyb_conv_w", "hyb_w_out", "pool_w", "pool_scale"]


def kernel(**inputs):
    import concourse.bacc as bacc
    from concourse.bass_utils import run_bass_kernel_spmd as run

    nc = bacc.Bacc("TRN2", target_bir_lowering=False, num_devices=1)
    arrays, aps = {}, {}
    for name in _INS + ["consts"]:
        a = shape_constants() if name == "consts" else np.ascontiguousarray(inputs[name])
        arrays[f"in_{name}"] = a
        aps[name] = nc.dram_tensor(f"in_{name}", a.shape, mybir.dt.from_np(a.dtype), kind="ExternalInput").ap()
    out = nc.dram_tensor("out_0", (1, T, D), F32, kind="ExternalOutput").ap()
    build(nc, aps, out)
    return run(nc, [arrays], core_ids=[0]).results[0]["out_0"]
```

```python
from contextlib import ExitStack

import numpy as np

import concourse.bass as bass
from concourse import mybir

F32 = mybir.dt.float32
F32R = mybir.dt.float32r
BF16 = mybir.dt.bfloat16
I32 = mybir.dt.int32
ALU = mybir.AluOpType
ACT = mybir.ActivationFunctionType
AX_X = mybir.AxisListType.X

P = 128
T = 512
D = 1024
KD = D // P
F = 2816
KF = F // P
KH2 = KF // 2
DH = 64
HEADS = 8
NQ = 4
NC = 31
NCP = 32
EPS = 1e-6
NEG = -1e30
TE = T + 16
PW = 2 * TE

COL_Q, COL_KC, COL_VC, COL_KS, COL_VS, COL_KW, COL_VW, COL_G = 0, 512, 640, 768, 896, 1024, 1152, 1280
COL_U = COL_G + 24
COL_GB = COL_U + 512
COL_GC = COL_GB + 512

U_FFN = {0: 0}
U_MIX = U_FFN[0] + 2 * KF + 2 * KD
U_W1 = U_MIX + 7
U_LOOP = U_W1 + 4
U_OUT = U_LOOP + 16
U_FFN[1] = U_OUT + KD
U_FFN[2] = U_FFN[1] + 2 * KF + 2 * KD
U_POOL = U_FFN[2] + 2 * KF + 2 * KD
U_FFN[3] = U_POOL + 4
U_END = U_FFN[3] + 2 * KF + 2 * KD

BLOCKS = [KD] * U_END
DMAS = [1] * U_END
for ffn in range(4):
    for u in range(2 * KD):
        BLOCKS[U_FFN[ffn] + 2 * KF + u] = KH2
for u in range(4):
    BLOCKS[U_POOL + u] = 4
    DMAS[U_LOOP + 4 * u] = 2
for u in range(KD):
    DMAS[U_OUT + u] = 3


def landed_by(n):
    return 16 * sum(DMAS[m] for m in range(n % 4, n + 1, 4))


XG_OF = {version: version for version in range(6)}
POOL_ORDER = (0, 3, 1, 2)
LATE = NQ


def tile_order(version):
    return [*range(LATE, KD - 1), *range(LATE), KD - 1] if version == 2 else [*range(KD)]


STATS = ["x0", "x1", "ks", "kw", "q0", "q1", "q2", "kc", "q3", "x2", "x3", "x4", "x5"]
AUX = ["gains", "rows", "pos", "rot_ks", "rot_kw", "t_vs", "t_vw", "t_gates", "rot_q0", "rot_q1", "rot_q2", "w2", "rot_kc",
       "t_vc", "rot_q3"]
LAST_P = 24

OUT_AFTER = ((0, 1), (2, 3), (4, 5), (6, 7))
OUT_PARTS = ((0, 2), (2, 4), (4, 6), (6, 7), (7, 8))

R_FFN, R_MIX, R_PSC, R_CONV, R_QN, R_KN, R_POS, N_ROWS = 0, 32, 48, 56, 68, 69, 72, 104

C_ID, C_ONE, C_BLK, C_ROT, C_MASK = 0, 128, 256, 384, 512
C_CMASK = 640
C_FREQ = 768
C_VALID = 769
C_POOL = 770
N_CONST = C_POOL + 64


def shape_constants():
    c = np.zeros((P, N_CONST), np.float32)
    r = np.arange(P)
    c[:, C_ID:C_ID + P] = np.eye(P)
    c[:, C_ONE:C_ONE + P] = 1.0
    c[:, C_BLK:C_BLK + P] = (r[:, None] // DH == r[None, :] // DH)
    for d in range(P):
        if d % DH < 8:
            c[d + 8, C_ROT + d] = -1.0
        elif d % DH < 16:
            c[d - 8, C_ROT + d] = 1.0
        if d % DH < 16:
            c[d, C_FREQ] = 500000.0 ** (-(d % 8) * 2 / 16)
    c[:, C_MASK:C_MASK + P] = np.where(r[None, :] > r[:, None], NEG, 0.0)
    n = np.arange(NCP)
    for q in range(NQ):
        bad = (16 * n[None, :] + 31 > q * P + r[:, None]) | (n[None, :] >= NC)
        c[:, C_CMASK + q * NCP:C_CMASK + (q + 1) * NCP] = np.where(bad, NEG, 0.0)
    c[:, C_VALID] = r >= 31
    c[:, C_POOL] = 0.0
    c[:, C_POOL + 1:C_POOL + 16] = 1.0
    for g, w in ((1, 4), (2, 8), (3, 16)):
        c[:, C_POOL + 16 * g:C_POOL + 16 * g + 16] = w / np.minimum(np.arange(16) + 1, w)
    return c


def circle_parts():
    out, rest = [], 2 * np.pi
    for bits in (9, 20):
        part = np.floor(rest * 2.0 ** bits) / 2.0 ** bits
        out.append(float(part))
        rest -= part
    return out + [float(np.float32(rest))]


PI_PARTS = circle_parts()
ROUND = 1.5 * 2.0 ** 23


def at_least(eng, sem, value):
    if isinstance(value, int) and value <= 0:
        return
    eng.wait_ge(sem, value)


def build(nc, A, out):
    with ExitStack() as ctx:
        def sb(name, shape, dt=F32, where=ctx):
            return where.enter_context(nc.sbuf_tensor(name, shape, dt))

        def sem(name):
            return ctx.enter_context(nc.semaphore(name))

        consts = sb("consts", [P, N_CONST])
        ident_b = sb("ident_b", [P, P], BF16)
        ones_r = sb("ones_r", [P, P], F32R)
        mask_b = sb("mask_b", [P, P + NQ * NCP], BF16)
        cols = sb("cols", [P, N_ROWS])
        x_t = sb("x_t", [P, KD * T])
        with ExitStack() as before_output:
            xg_hi = sb("xg_hi", [P, KD * T], F32R, before_output)
        out_rows = sb("out_rows", [P, NQ, D])
        xg_lo = sb("xg_lo", [P, KD * T], F32R)
        raw = sb("raw", [P, 4, KH2 * P])
        w_hi = sb("w_hi", [P, 2, KH2 * P], F32R)
        w_lo = sb("w_lo", [P, 2, KH2 * P], F32R)
        with ExitStack() as at_sums:
            ss_parts = sb("ss_parts", [P, 2, T], F32R, at_sums)
        work = sb("work", [P, 2, T])
        scratch = sb("scratch", [P, 4, T])
        work2, sq, ss, ms = (scratch[:, i, :] for i in range(4))
        rstd = sb("rstd", [P, T])
        cos_t = sb("cos_t", [P, TE])
        sin_t = sb("sin_t", [P, TE])
        w2_raw = sb("w2_raw", [P, 2, 2, DH])
        half = sb("half", [P, 1])
        ang, turns, step_ = sin_t[:, 0:T], cos_t[:, 0:T], ss[:, :]
        eps_col = sb("eps_col", [P, 1])

        with ExitStack() as once:
            rows = sb("rows", [N_ROWS, P], F32, once)
            x_in = sb("x_in", [P, NQ, D], F32, once)
            pos_i = sb("pos_i", [1, T], I32, once)
            pos_f = sb("pos_f", [1, T], F32, once)
        with ExitStack() as ffn_ctx:
            act_hi = sb("act_hi", [P, KF * T], F32R, ffn_ctx)
            act_lo = sb("act_lo", [P, KF * T], F32R, ffn_ctx)
        with ExitStack() as mix_ctx:
            def mb(name, shape, dt=F32):
                return sb(name, shape, dt, mix_ctx)
            qf = mb("qf", [P, NQ * T])
            q_parts = mb("q_parts", [P, 2, T], F32R)
            k_hi = mb("k_hi", [P, 2, 2, T], F32R)
            k_lo = mb("k_lo", [P, 2, 2, T], F32R)
            kc_hi = mb("kc_hi", [P, 2, NCP], F32R)
            kc_lo = mb("kc_lo", [P, 2, NCP], F32R)
            v_hi = mb("v_hi", [P, 2, NQ * P], F32R)
            v_lo = mb("v_lo", [P, 2, NQ * P], F32R)
            vc_hi = mb("vc_hi", [NCP, P], F32R)
            vc_lo = mb("vc_lo", [NCP, P], F32R)
            ob_hi = mb("ob_hi", [P, 4 * T], F32R)
            ob_lo = mb("ob_lo", [P, 4 * T], F32R)
            prob = mb("prob", [P, 2, PW])
            pt_b = mb("pt_b", [P, 2, 4 * T], F32R)
            prob_c = mb("prob_c", [P, NQ, NCP])
            ptc = mb("ptc", [NCP, 2, T], F32R)
            m1 = mb("m1", [P, T])
            vt = mb("vt", [P, T])
            hid = mb("hid", [P, 2, 2, DH])
            hid_hi = mb("hid_hi", [P, 2, DH], F32R)
            hid_lo = mb("hid_lo", [P, 2, DH], F32R)
            kcv = mb("kcv", [P, 2, DH])
            kcm = mb("kcm", [P, 2, DH])
            gate = mb("gate", [P, 2, NQ * 24])
            small = mb("small", [P, 2, 10])
            small_c = mb("small_c", [P, 5, NQ])
            w2_hi, w2_lo = (q_parts[:, i, 0:2 * P].rearrange("p (c d) -> p c d", c=2) for i in range(2))
        with ExitStack() as pool_ctx:
            h_pad = sb("h_pad", [P, KD, TE], F32, pool_ctx)
            sums_v = [sb(f"sums_v{i}", [P, 2, TE], F32, pool_ctx) for i in range(2)]
            sums_p = [sb(f"sums_p{i}", [P, 2, TE], F32, pool_ctx) for i in range(2)]

        ps_s = ctx.enter_context(nc.psum_tensor("ps_s", [P, 4, T], F32))
        ps_y = ctx.enter_context(nc.psum_tensor("ps_y", [P, 2, T], F32))
        ps_stat = ctx.enter_context(nc.psum_tensor("ps_stat", [P, T], F32))
        ps_aux = ctx.enter_context(nc.psum_tensor("ps_aux", [P, T], F32))

        raw_landed = [sem(f"raw_landed{i}") for i in range(4)]
        const_landed = sem("const_landed")
        gains_landed = sem("gains_landed")
        rows_landed = sem("rows_landed")
        w2_landed = sem("w2_landed")
        x_landed = [sem(f"x_landed{i}") for i in range(NQ)]
        hi_ready = sem("hi_ready")
        lo_ready = sem("lo_ready")
        unit_done = sem("unit_done")
        rows_turned = sem("rows_turned")
        x_turned = sem("x_turned")
        consts_cast = sem("consts_cast")
        x_ready = sem("x_ready")
        xg_hi_ready = sem("xg_hi_ready")
        xg_lo_ready = sem("xg_lo_ready")
        sq_ready = sem("sq_ready")
        ss_step = sem("ss_step")
        ss_hi_ready = sem("ss_hi_ready")
        ss_lo_ready = sem("ss_lo_ready")
        stat_done = sem("stat_done")
        ms_ready = sem("ms_ready")
        root_ready = sem("root_ready")
        gate_scaled = sem("gate_scaled")
        up_scaled = sem("up_scaled")
        silu_ready = sem("silu_ready")
        a_ready = sem("a_ready")
        act_hi_ready = sem("act_hi_ready")
        act_lo_ready = sem("act_lo_ready")
        aux_done = sem("aux_done")
        aux_free = sem("aux_free")
        pos_ready = sem("pos_ready")
        pool_step = sem("pool_step")
        pos_landed = sem("pos_landed")
        pair_step = sem("pair_step")
        odd_ready = sem("odd_ready")
        max_step = sem("max_step")
        sum_step = sem("sum_step")
        pool_zeroed = sem("pool_zeroed")
        kc_hi_ready = sem("kc_hi_ready")
        conv_step = sem("conv_step")
        kc_ready = sem("kc_ready")
        turn_ready = sem("turn_ready")
        trig_ready = sem("trig_ready")
        mix_zeroed = sem("mix_zeroed")
        probs_zeroed = sem("probs_zeroed")
        proj_scaled = sem("proj_scaled")
        head_sq = sem("head_sq")
        gained = sem("gained")
        m1_ready = sem("m1_ready")
        rope_ready = sem("rope_ready")
        dve_step = sem("dve_step")
        k_hi_ready = sem("k_hi_ready")
        k_lo_ready = sem("k_lo_ready")
        v_hi_ready = sem("v_hi_ready")
        blk_step = sem("blk_step")
        blk_hi_ready = sem("blk_hi_ready")
        blk_lo_ready = sem("blk_lo_ready")
        w2_hi_ready = sem("w2_hi_ready")
        w2_lo_ready = sem("w2_lo_ready")
        gelu_in = sem("gelu_in")
        gelu_tanh = sem("gelu_tanh")
        hid_ready = sem("hid_ready")
        hid_hi_ready = sem("hid_hi_ready")
        hid_lo_ready = sem("hid_lo_ready")
        gate_exp = sem("gate_exp")
        ob_ready = sem("ob_ready")
        ob_hi_ready = sem("ob_hi_ready")
        ob_lo_ready = sem("ob_lo_ready")
        qp_hi_ready = sem("qp_hi_ready")
        qp_lo_ready = sem("qp_lo_ready")
        qk_done = sem("qk_done")
        negmax_ready = sem("negmax_ready")
        exp_done = sem("exp_done")
        scale_ready = sem("scale_ready")
        pt_done = sem("pt_done")
        c_qk_done = sem("c_qk_done")
        c_max_step = sem("c_max_step")
        c_negmax_ready = sem("c_negmax_ready")
        c_exp_done = sem("c_exp_done")
        c_sum_step = sem("c_sum_step")
        c_scale_ready = sem("c_scale_ready")
        c_p_scaled = sem("c_p_scaled")
        c_pt_done = sem("c_pt_done")
        c_pt_hi_ready = sem("c_pt_hi_ready")
        c_pt_lo_ready = sem("c_pt_lo_ready")
        pt_hi_ready = sem("pt_hi_ready")
        pt_lo_ready = sem("pt_lo_ready")
        pv_done = sem("pv_done")
        o_hi_ready = sem("o_hi_ready")
        o_lo_ready = sem("o_lo_ready")
        y_copied = sem("y_copied")
        z_ready = sem("z_ready")
        less_z = sem("less_z")
        out_turned = sem("out_turned")
        out_copied = sem("out_copied")
        out_stored = sem("out_stored")

        ident = consts[:, C_ID:C_ID + P]
        ones = consts[:, C_ONE:C_ONE + P]
        block_ones = consts[:, C_BLK:C_BLK + P]
        rot = consts[:, C_ROT:C_ROT + P]
        freq = consts[:, C_FREQ:C_FREQ + 1]

        def tile_of(tensor, d):
            return tensor[:, bass.ds(d * T, T)]

        def square_of(d):
            return scratch[:, 1 - d % 2, :]

        def head_tiles(name):
            return STATS.index(name) - STATS.index("ks") + 1

        def turned_parts(slot_):
            if slot_:
                return pt_b[:, 0, :], pt_b[:, 1, :]
            return xg_hi[:, 4 * T:8 * T], xg_lo[:, 4 * T:8 * T]

        def prob_of(s):
            if s % 4 < 2:
                return prob[:, s % 4, :]
            return scratch[:, 2 * (s % 4) - 4:2 * (s % 4) - 2, :].rearrange("p b k -> p (b k)")

        def diagonal(s, br):
            return work[:, s % 2, br * P:(br + 1) * P]

        def f32(ap):
            return ap.bitcast(F32)

        def normed(tt, g):
            z = h_pad[:, 2 * g:2 * g + 2, 16:TE]
            return tt(z, z, rstd[:, :].unsqueeze(1).to_broadcast([P, 2, T]), ALU.mult)

        def window_sum(tt, then, g, buffers):
            src = h_pad[:, 2 * g:2 * g + 2, :]
            for level in range(g + 1):
                dst, back = buffers[level % 2], 1 << level
                then(tt(dst[:, :, 16:TE], src[:, :, 16 - back:TE - back], src[:, :, 16:TE],
                        ALU.add if g else ALU.subtract))
                src = dst
            then(tt(src[:, :, 16:32], src[:, :, 16:32],
                    consts[:, C_POOL + 16 * g:C_POOL + 16 * g + 16].unsqueeze(1).to_broadcast([P, 2, 16]), ALU.mult))
            return src

        def x_less_z(tt, g):
            x = x_t[:, 2 * g * T:(2 * g + 2) * T].rearrange("p (k t) -> p k t", k=2)
            return tt(x, x, h_pad[:, 2 * g:2 * g + 2, 16:TE], ALU.subtract)

        block = ctx.enter_context(nc.Block())

        @block.sync
        def _(sp):
            for q in range(NQ):
                sp.dma_start(x_in[:, q, :], A["x"][0, q * P:(q + 1) * P, :]).then_inc(x_landed[q], 16)

            def load(n, i, *parts):
                at_least(sp, lo_ready, n - 3 + 4 * i)
                for dst, src in parts:
                    sp.dma_start(dst, src).then_inc(raw_landed[n % 4], 16)

            def slot(n, blocks=KD):
                return raw[:, n % 4, 0:blocks * P].rearrange("p (k f) -> p k f", f=P)

            def blocks_of(w):
                return w.rearrange("(k p) f -> p k f", p=P)

            def load_up(ffn, i):
                for u in range(4):
                    n, f = U_FFN[ffn] + u, 2 * i + u // 2
                    w = A["ffn_w_up" if u % 2 else "ffn_w_gate"][ffn // 2, ffn % 2]
                    load(n, i, (slot(n), blocks_of(w[:, bass.ds(f * P, P)])))

            def load_down(ffn, i):
                for u in range(4):
                    n, d, h = U_FFN[ffn] + 2 * KF + u, 2 * i + u // 2, u % 2
                    w = A["ffn_w_down"][ffn // 2, ffn % 2]
                    load(n, i, (slot(n, KH2), blocks_of(w[h * KH2 * P:(h + 1) * KH2 * P, bass.ds(d * P, P)])))

            def load_ffn(ffn):
                load_up(ffn, 0)
                with sp.Fori(1, KF // 2) as i:
                    load_up(ffn, i)
                with sp.Fori(0, KD // 2) as i:
                    load_down(ffn, i)

            load_ffn(0)
            w_in = A["hyb_w_in"][0]
            for u, col in enumerate((COL_KS, COL_KW, COL_KC, COL_VC, COL_VS, COL_VW, COL_G)):
                load(U_MIX + u, 0, (slot(U_MIX + u), blocks_of(w_in[:, col:col + P])))
            for u in range(4):
                w1 = A["hyb_cmp_w1"][0, u // 2][(u % 2) * KD * P:(u % 2 + 1) * KD * P, :]
                load(U_W1 + u, 0, (slot(U_W1 + u), blocks_of(w1)))
            with sp.Fori(0, 4) as i:
                for u, col in enumerate((COL_Q, COL_U, COL_GC, COL_GB)):
                    n = U_LOOP + u
                    if u == 0:
                        load(n, i, *((slot(n)[:, :, g * DH:(g + 1) * DH],
                                      blocks_of(w_in[:, bass.ds(i * DH + g * 4 * DH, DH)])) for g in range(2)))
                    else:
                        load(n, i, (slot(n), blocks_of(w_in[:, bass.ds(i * P + col, P)])))
            w_out = A["hyb_w_out"][0]
            for d in range(KD):
                n = U_OUT + d
                w = w_out[:, d * P:(d + 1) * P]
                load(n, 0, *((slot(n)[g * DH:(g + 1) * DH, 0:4, :],
                              w[g * 4 * DH:(g + 1) * 4 * DH, :].rearrange("(j p) f -> p j f", p=DH)) for g in range(2)),
                     (slot(n)[:, 4:8, :], blocks_of(w[T:2 * T, :])))
            load_ffn(1)
            load_ffn(2)
            for u, g in enumerate(POOL_ORDER):
                n = U_POOL + u
                load(n, 0, (raw[:, n % 4, 0:4 * P].rearrange("p (k f) -> p k f", k=2), blocks_of(A["pool_w"][0, g])))
            load_ffn(3)
            for first, end in OUT_PARTS:
                sp.wait_ge(out_copied, end)
                sp.dma_start(out[0, :, first * P:end * P].rearrange("(q p) f -> p q f", p=P),
                             out_rows[:, :, first * P:end * P]).then_inc(out_stored, 16)
            sp.wait_ge(out_stored, 16 * len(OUT_PARTS))

        @block.tensor
        def _(pe):
            mm = nc.tensor.matmul

            def three(bank, hi, lo, x_hi, x_lo, first, last, **kw):
                mm(bank, hi, x_hi, start=first, stop=False, **kw)
                mm(bank, hi, x_lo, start=False, stop=False, **kw)
                return mm(bank, lo, x_hi, start=False, stop=last, **kw)

            def stat(index, weights, source, cols_=T):
                at_least(pe, ms_ready, index)
                mm(ps_stat[:, 0:cols_], weights, source, start=True, stop=True).then_inc(stat_done, 1)

            def total_stat(version):
                pe.wait_ge(ss_lo_ready, version + 1)
                at_least(pe, ms_ready, STATS.index(f"x{version}"))
                mm(ps_stat[:, :], ones_r[:, :], ss_parts[:, 0, :], start=True, stop=False)
                mm(ps_stat[:, :], ones_r[:, :], ss_parts[:, 1, :], start=False, stop=True).then_inc(stat_done, 1)

            def unit(n, i, bank, x_hi, x_lo, k0=0, first=True, last=True, version=None, midway=None):
                pe.wait_ge(lo_ready, n + 1 + 4 * i)
                order = range(BLOCKS[n]) if version is None else tile_order(version)
                for place, k in enumerate(order):
                    if midway and place == midway[0]:
                        midway[1]()
                    if version is not None:
                        pe.wait_ge(xg_lo_ready, KD * XG_OF[version] + place + 1)
                    last_mm = three(bank, w_hi[:, n % 2, k * P:(k + 1) * P], w_lo[:, n % 2, k * P:(k + 1) * P],
                                    tile_of(x_hi, k0 + k), tile_of(x_lo, k0 + k),
                                    first and place == 0, last and place == BLOCKS[n] - 1)
                last_mm.then_inc(unit_done, 1)

            def up(ffn, version, i, peeled):
                for u in range(4):
                    n, f = U_FFN[ffn] + u, 2 * i + u // 2
                    at_least(pe, up_scaled if u % 2 else gate_scaled, KF * ffn + f - 1)
                    fresh = peeled and u == 0
                    unit(n, i, ps_s[:, (u % 2) * 2 + u // 2, :], xg_hi, xg_lo, version=version if fresh else None,
                         midway=(4, lambda: total_stat(version)) if peeled and u == 1 else None)
                    if fresh:
                        if version == 0:
                            pe.wait_ge(aux_free, AUX.index("pos"))
                            pe.wait_ge(pos_ready, 1)
                            mm(ps_aux[:, :], ones[0:1, :], pos_f[0:1, :], start=True, stop=True).then_inc(aux_done, 1)

            def down(ffn, version_out, i, leaving=False):
                for u in range(4):
                    n, d, h = U_FFN[ffn] + 2 * KF + u, 2 * i + u // 2, u % 2
                    if h == 0:
                        pe.wait_ge(x_ready, KD * version_out + d - 1)
                    pe.wait_ge(act_lo_ready, KF * ffn + (h + 1) * KH2)
                    unit(n, i, ps_y[:, u // 2, :], act_hi, act_lo, k0=h * KH2, first=(h == 0), last=(h == 1))
                    if leaving:
                        for o in OUT_AFTER[u]:
                            leave(o)

            def leave(d):
                pe.wait_ge(x_ready, KD * 6 + d + 1)
                at_least(pe, out_copied, d - 3)
                for q in range(NQ):
                    t = nc.tensor.transpose(ps_s[:, d % 4, q * P:(q + 1) * P], x_t[:, d * T + q * P:d * T + (q + 1) * P],
                                            ident)
                t.then_inc(out_turned, 1)

            def run_ffn(ffn, version, version_out):
                up(ffn, version, 0, True)
                with pe.Fori(1, KF // 2) as i:
                    up(ffn, version, i, False)
                with pe.Fori(0, KD // 2 - (ffn == 3)) as i:
                    down(ffn, version_out, i)
                if ffn == 3:
                    down(ffn, version_out, KD // 2 - 1, leaving=True)

            pe.wait_ge(const_landed, 16)
            pe.wait_ge(gains_landed, 16)
            nc.tensor.transpose(ps_aux[:, 0:R_MIX], rows[0:R_MIX, :], ident[0:R_MIX, 0:R_MIX]).then_inc(aux_done, 1)
            banks = [ps_s[:, 0, :], ps_s[:, 1, :], ps_s[:, 2, :], ps_s[:, 3, :], ps_y[:, 0, :], ps_y[:, 1, :],
                     ps_stat[:, :], ps_s[:, 1, :]]

            def turn_x(d, q):
                return nc.tensor.transpose(banks[d][:, q * P:(q + 1) * P], x_in[:, q, d * P:(d + 1) * P], ident)

            for q in range(NQ):
                pe.wait_ge(x_landed[q], 16)
                for d in range(KD - 1):
                    turned = turn_x(d, q)
                    if q == NQ - 1:
                        turned.then_inc(x_turned, 1)
            pe.wait_ge(x_ready, 2)
            for q in range(NQ):
                turned = turn_x(KD - 1, q)
            turned.then_inc(x_turned, 1)
            pe.wait_ge(rows_landed, 16 * 8)
            pe.wait_ge(aux_free, 1)
            nc.tensor.transpose(ps_aux[:, 0:N_ROWS], rows[:, :], ident[0:N_ROWS, 0:N_ROWS]).then_inc(aux_done, 1)

            run_ffn(0, 0, 1)

            def project(n, i, p, **kw):
                at_least(pe, proj_scaled, p - 3 + 4 * i)
                unit(n, i, ps_y[:, 0, :] if p == LAST_P else ps_s[:, p % 4, :], xg_hi, xg_lo, **kw)

            def aux_start(name, i=0):
                pe.wait_ge(aux_free, AUX.index(name) + i)

            def head_stat(name, tile, i=0):
                pe.wait_ge(head_sq, head_tiles(name) + i)
                pe.wait_ge(ms_ready, STATS.index(name) + i)
                mm(ps_stat[:, :], block_ones, tile, start=True, stop=True).then_inc(stat_done, 1)

            def rotate(name, slot_, i=0):
                aux_start("rot_" + name, i)
                pe.wait_ge(gained, head_tiles(name) + i)
                mm(ps_aux[:, :], rot, work[:, slot_, :], start=True, stop=True).then_inc(aux_done, 1)

            def turn_vt(name, count, rows_):
                aux_start(name)
                pe.wait_ge(proj_scaled, count)
                for q in range(NQ):
                    t = nc.tensor.transpose(ps_aux[:, q * rows_:(q + 1) * rows_], vt[0:rows_, q * P:(q + 1) * P],
                                            ident[0:rows_, 0:rows_])
                t.then_inc(aux_done, 1)

            def compress(c):
                p = 7 + c
                pe.wait_ge(proj_scaled, p - 3)
                pe.wait_ge(blk_lo_ready, c + 1)
                for h in range(2):
                    n = U_W1 + 2 * c + h
                    pe.wait_ge(lo_ready, n + 1)
                    for k in range(KD):
                        at = (h * KD + k) * 2 * NCP
                        b_hi, b_lo = (pt_b[:, c, part + at:part + at + 2 * NCP].unsqueeze(1).to_broadcast([P, 4, 2 * NCP])
                                      for part in (0, 2 * T))
                        last_mm = three(ps_s[:, p % 4, 0:8 * NCP],
                                        w_hi[:, n % 2, k * P:(k + 1) * P], w_lo[:, n % 2, k * P:(k + 1) * P],
                                        b_hi, b_lo, h == 0 and k == 0, h == 1 and k == KD - 1)
                    last_mm.then_inc(unit_done, 1)

            project(U_MIX, 0, 0, version=1)
            project(U_MIX + 1, 0, 1, midway=(2, lambda: total_stat(1)))
            project(U_MIX + 2, 0, 2)
            head_stat("ks", sq[:, :])
            project(U_MIX + 3, 0, 3)
            head_stat("kw", sq[:, :])
            rotate("ks", 0)
            project(U_MIX + 4, 0, 4)
            rotate("kw", 1)
            project(U_MIX + 5, 0, 5)
            turn_vt("t_vs", 5, P)
            project(U_MIX + 6, 0, 6)
            turn_vt("t_vw", 6, P)
            compress(0)
            turn_vt("t_gates", 7, 24)
            compress(1)

            def project_four(b, i, extra=None):
                for u in range(4):
                    project(U_LOOP + 4 * b + u, i, 9 + 4 * b + u,
                            midway=(5, lambda: head_stat("q3" if b else "q0", sq[:, :], i)) if u == 1 else
                            (5, first_scores) if u == 3 and b else None)
                    if u == 0 and extra:
                        extra[0]()
                    if u == 1 and extra:
                        extra[1]()
                    if u == 2:
                        if extra:
                            extra[2]()
                        rotate("q3" if b else "q0", 0, i)

            with pe.Fori(0, 3) as i:
                project_four(0, i)

            aux_start("w2")
            pe.wait_ge(w2_lo_ready, 1)
            for c in range(2):
                pe.wait_ge(hid_lo_ready, c + 1)
                last_mm = three(ps_aux[:, c * 2 * NCP:(c + 1) * 2 * NCP], w2_hi[:, c, :], w2_lo[:, c, :],
                                hid_hi[:, c, :], hid_lo[:, c, :], True, True)
            last_mm.then_inc(aux_done, 1)

            def kc_stat():
                pe.wait_ge(head_sq, head_tiles("kc"))
                pe.wait_ge(ms_ready, STATS.index("kc"))
                mm(ps_stat[:, 0:2 * NCP], block_ones, kcm[:, 0, :], start=True, stop=True).then_inc(stat_done, 1)

            def kc_rotate():
                aux_start("rot_kc")
                pe.wait_ge(gained, head_tiles("kc"))
                mm(ps_aux[:, 0:2 * NCP], rot, kcv[:, 0, :], start=True, stop=True).then_inc(aux_done, 1)

            def vc_turn():
                aux_start("t_vc")
                for g in range(2):
                    t = nc.tensor.transpose(ps_aux[0:NCP, g * DH:(g + 1) * DH], kcv[0:DH, 1, g * NCP:(g + 1) * NCP],
                                            ident[0:DH, 0:DH])
                t.then_inc(aux_done, 1)

            def scores(j, s):
                j, s = j + s // 8, s % 8
                g, c = s // 4, s % 4
                width = (c + 1) * P
                pe.wait_ge(qp_lo_ready, 2 * j + g + 1)
                at_least(pe, exp_done, 8 * j + s - 1)
                query = q_parts[:, g, c * P:(c + 1) * P]
                wide = max(width, 2 * P)
                for br in range(2):
                    bank = ps_s[:, 2 * (s % 2) + br, :]
                    mm(bank[:, 0:wide], query, k_hi[:, br, g, 0:wide], start=True, stop=False)
                    mm(bank[:, c * P:width], ident_b[:, :], mask_b[:, 0:P], start=False, stop=False)
                    last_mm = mm(bank[:, 0:wide], query, k_lo[:, br, g, 0:wide], start=False, stop=True)
                last_mm.then_inc(qk_done, 1)

            def scores_c(j, g):
                pe.wait_ge(qp_lo_ready, 2 * j + g + 1)
                if g or not isinstance(j, int):
                    pe.wait_ge(c_pt_lo_ready, 2 * j + g)
                for c in range(NQ):
                    bank = ps_stat[:, c * NCP:(c + 1) * NCP]
                    query = q_parts[:, g, c * P:(c + 1) * P]
                    mm(bank, query, kc_hi[:, g, :], start=True, stop=False)
                    mm(bank, ident_b[:, :], mask_b[:, P + c * NCP:P + (c + 1) * NCP], start=False, stop=False)
                    last_mm = mm(bank, query, kc_lo[:, g, :], start=False, stop=True)
                last_mm.then_inc(c_qk_done, 1)

            def turn_c(j, g):
                pe.wait_ge(c_p_scaled, 2 * j + g + 1)
                for c in range(NQ):
                    t = nc.tensor.transpose(ps_stat[0:NCP, c * P:(c + 1) * P], prob_c[:, c, :], ident)
                t.then_inc(c_pt_done, 1)

            def turn(j, s):
                c = s % 4
                pe.wait_ge(scale_ready, 8 * j + s + 1)
                at_least(pe, pt_lo_ready, 8 * j + s)
                for br in range(2):
                    for k in range(c + 1):
                        at = br * T + k * P
                        t = mm(ps_y[:, br, k * P:(k + 1) * P], prob_of(s)[:, at:at + P], diagonal(s, br),
                               start=True, stop=True)
                t.then_inc(pt_done, 1)

            def values(j, pair):
                j, pair = j + pair // 4, pair % 4
                pe.wait_ge(pt_lo_ready, 8 * j + 2 * pair + 2)
                bank = ps_aux[:, (pair % 2) * 2 * P:(pair % 2 + 1) * 2 * P]
                half_pair = pair % 2
                p_hi, p_lo = turned_parts(pair % 2)
                queries = slice(pair % 2 * 2 * P, (pair % 2 + 1) * 2 * P)
                pe.wait_ge(c_pt_lo_ready, 2 * j + pair // 2 + 1)
                three(bank, vc_hi[:, :], vc_lo[:, :], ptc[:, 0, queries], ptc[:, 1, queries], True, False)
                for br in range(2):
                    for k in range(2 * half_pair + 2):
                        at = (br * 4 + k) * 2 * P
                        last_mm = three(bank, v_hi[:, br, k * P:(k + 1) * P], v_lo[:, br, k * P:(k + 1) * P],
                                        p_hi[:, at:at + 2 * P], p_lo[:, at:at + 2 * P],
                                        False, br == 1 and k == 2 * half_pair + 1)
                last_mm.then_inc(pv_done, 1)

            def attend(j, first=False, last=False):
                for s in range(8):
                    if not (last and s + 2 >= 8):
                        scores(j, s + 2)
                    if first and s == 3:
                        pe.wait_ge(probs_zeroed, 1)
                    if s % 2 and not (first and s == 1):
                        values(j, (s - 3) // 2)
                    if s in (2, 6):
                        turn_c(j, s // 4)
                    turn(j, s)
                    if s in (3, 7) and not (last and s == 7):
                        scores_c(j + s // 7, 1 - s // 7)

            def first_scores():
                pe.wait_ge(proj_scaled, LAST_P)
                pe.wait_ge(ms_ready, STATS.index("q3") + 1)
                pe.wait_ge(kc_ready, 1)
                pe.wait_ge(k_lo_ready, 2)
                pe.wait_ge(consts_cast, 2)
                scores(0, 0)
                scores_c(0, 0)
                scores(0, 1)

            project_four(3, 0, (kc_stat, kc_rotate, vc_turn))
            pe.wait_ge(proj_scaled, LAST_P + 1)
            pe.wait_ge(aux_free, len(AUX))
            attend(0, first=True)
            with pe.Fori(1, 3) as j:
                attend(j)
            attend(3, last=True)

            def from_conv(d):
                n = U_OUT + d
                at_least(pe, x_ready, KD * 2 + d - 1 if d > 1 else 0)
                pe.wait_ge(lo_ready, n + 1)
                for k in range(4, KD):
                    three(ps_s[:, 2 + d % 2, :], w_hi[:, n % 2, k * P:(k + 1) * P], w_lo[:, n % 2, k * P:(k + 1) * P],
                          tile_of(ob_hi, k - 4), tile_of(ob_lo, k - 4), k == 4, False)

            def from_attention(d):
                n = U_OUT + d
                for k in range(4):
                    last_mm = three(ps_s[:, 2 + d % 2, :], w_hi[:, n % 2, k * P:(k + 1) * P],
                                    w_lo[:, n % 2, k * P:(k + 1) * P],
                                    tile_of(xg_hi, k), tile_of(xg_lo, k), False, k == 3)
                last_mm.then_inc(unit_done, 1)

            from_conv(0)
            values(3, 3)
            from_conv(1)
            pe.wait_ge(o_lo_ready, 16)
            from_attention(0)
            from_attention(1)
            for d in range(2, KD):
                from_conv(d)
                from_attention(d)

            run_ffn(1, 2, 3)
            run_ffn(2, 3, 4)

            banks = [ps_s[:, 0, :], ps_s[:, 1, :], ps_s[:, 2, :], ps_s[:, 3, :], ps_y[:, 0, :], ps_y[:, 1, :],
                     ps_aux[:, :], ps_stat[:, :]]
            for u, g in enumerate(POOL_ORDER):
                n = U_POOL + u
                pe.wait_ge(lo_ready, n + 1)
                pe.wait_ge(xg_lo_ready, KD * XG_OF[4] + 2 * g + 2)
                if u == 2:
                    pe.wait_ge(x_ready, KD * 5)
                if u == 3:
                    pe.wait_ge(ms_ready, STATS.index("x4") + 1)
                for o in range(2):
                    for k in range(2):
                        at = (2 * k + o) * P
                        last_mm = three(banks[2 * u + o], w_hi[:, n % 2, at:at + P], w_lo[:, n % 2, at:at + P],
                                        tile_of(xg_hi, 2 * g + k), tile_of(xg_lo, 2 * g + k), k == 0, k == 1)
                last_mm.then_inc(unit_done, 1)
                if u == 1:
                    total_stat(4)

            run_ffn(3, 5, 6)
        @block.scalar
        def _(act):
            def copy(dst, src):
                return nc.scalar.copy(dst, src)

            def split(n, i=0):
                at_least(act, unit_done, n - 1 + 4 * i)
                act.wait_ge(raw_landed[n % 4], landed_by(n) + 16 * DMAS[n] * i)
                copy(w_hi[:, n % 2, 0:BLOCKS[n] * P], raw[:, n % 4, 0:BLOCKS[n] * P]).then_inc(hi_ready, 1)

            def xg_high(d, gain):
                nc.scalar.activation(tile_of(xg_hi, d), tile_of(x_t, d), ACT.Copy,
                                     scale=cols[:, bass.ds(gain + d, 1)]).then_inc(xg_hi_ready, 1)

            def take_x(version, d, gain, odd=None):
                at_least(act, ss_step, KD * version + d - 1)
                act.wait_ge(x_ready, KD * version + d + 1)
                if gain is not None:
                    xg_high(d, gain)
                nc.scalar.activation(square_of(d % 2 if odd is None else odd), tile_of(x_t, d),
                                     ACT.Square).then_inc(sq_ready, 1)

            def sums_high(version):
                act.wait_ge(ss_step, KD * (version + 1))
                copy(ss_parts[:, 0, :], ss[:, :]).then_inc(ss_hi_ready, 1)

            def root(name, width, cols_=T, i=0):
                index = STATS.index(name) + i
                act.wait_ge(stat_done, index + 1)
                at_least(act, root_ready, index)
                nc.scalar.activation(ms[:, 0:cols_], ps_stat[:, 0:cols_], ACT.Sqrt, scale=1.0 / width,
                                     bias=eps_col[:, :]).then_inc(ms_ready, 1)

            def up(ffn, b, i, first=False):
                for u in range(4):
                    f = 2 * (b + i) + u // 2
                    if first and u < 2:
                        if u == 0:
                            split(U_FFN[ffn] + 3)
                    else:
                        split(U_FFN[ffn] + 4 * b + u + 2, i)
                    if u % 2 == 0:
                        act.wait_ge(gate_scaled, KF * ffn + f + 1)
                        nc.scalar.activation(work[:, u // 2, :], work[:, u // 2, :], ACT.Silu).then_inc(silu_ready, 1)
                    else:
                        act.wait_ge(a_ready, KF * ffn + f + 1)
                        copy(tile_of(act_hi, f), work[:, u // 2, :]).then_inc(act_hi_ready, 1)

            def down(ffn, version_out, gain, b, i, last=False):
                for u in range(4):
                    d = 2 * (b + i) + u // 2
                    n = U_FFN[ffn] + 2 * KF + 4 * b + u + 2
                    if n < U_END:
                        split(n, i)
                    if u % 2 and version_out < 6:
                        take_x(version_out, d, gain, u // 2)

            def run_ffn(ffn, version, version_out, gain):
                sums_high(version)
                split(U_FFN[ffn] + 2)
                root(f"x{version}", D)
                nc.scalar.preload_act_table(ACT.Silu)
                up(ffn, 0, 0, first=True)
                with act.Fori(1, KF // 2 - 1) as i:
                    up(ffn, 0, i)
                up(ffn, KF // 2 - 1, 0)
                if ffn == 0:
                    rope_tables()
                with act.Fori(0, KD // 2 - 1) as i:
                    down(ffn, version_out, gain, 0, i)
                down(ffn, version_out, gain, KD // 2 - 1, 0)

            def rope_tables():
                act.wait_ge(turn_ready, 1)
                nc.scalar.activation(turns, ang, ACT.Abs).then_inc(trig_ready, 1)
                nc.scalar.activation(sin_t[:, 0:T], ang, ACT.Sin).then_inc(trig_ready, 1)
                act.wait_ge(trig_ready, 2)
                nc.scalar.activation(cos_t[:, 0:T], turns, ACT.Sin, scale=-1.0,
                                     bias=half[:, :]).then_inc(trig_ready, 1)

            act.dma_start(rows[R_FFN:R_MIX, :], A["ffn_norm"].rearrange("l h (k p) -> (l h k) p", p=P)).then_inc(gains_landed, 16)
            act.dma_start(consts[:, :], A["consts"]).then_inc(const_landed, 16)
            act.dma_start(rows[R_MIX:R_PSC, :], A["mix_norm"].rearrange("l (k p) -> (l k) p", p=P)).then_inc(rows_landed, 16)
            act.dma_start(rows[R_PSC:R_CONV, :], A["pool_scale"].rearrange("l (k p) -> (l k) p", p=P)).then_inc(rows_landed, 16)
            act.dma_start(rows[R_CONV:R_QN, :], A["hyb_conv_w"].rearrange("l i (k p) -> (l i k) p", p=P)).then_inc(rows_landed, 16)
            for g in range(2):
                act.dma_start(rows[R_QN:R_KN, g * DH:(g + 1) * DH], A["hyb_q_norm"]).then_inc(rows_landed, 16)
                act.dma_start(rows[R_KN:R_POS, g * DH:(g + 1) * DH], A["hyb_k_norm"][0]).then_inc(rows_landed, 16)
            act.dma_start(rows[R_POS:N_ROWS, :], A["hyb_cmp_pos"].rearrange("l c (j e) d -> (l c j) (e d)", e=2)).then_inc(rows_landed, 16)
            act.dma_start(pos_i[:, :], A["positions"]).then_inc(pos_landed, 16)
            for g in range(2):
                act.dma_start(w2_raw[:, :, g, :], A["hyb_cmp_w2"][0].rearrange("c h d -> h c d")).then_inc(w2_landed, 16)
            act.wait_ge(const_landed, 16)
            copy(ones_r[:, :], ones)
            act.wait_ge(aux_free, 1)
            for d in range(KD):
                take_x(0, d, R_FFN)
                if d in (0, 2):
                    split(d // 2)
            copy(ident_b[:, :], ident).then_inc(consts_cast, 1)
            copy(mask_b[:, :], consts[:, C_MASK:C_CMASK + NQ * NCP]).then_inc(consts_cast, 1)
            run_ffn(0, 0, 1, R_MIX)

            def square(name, dst, src, i=0):
                act.wait_ge(stat_done, STATS.index(name) + i)
                nc.scalar.activation(dst, src, ACT.Square).then_inc(head_sq, 1)

            def split_keys(br):
                act.wait_ge(rope_ready, head_tiles("ks") + br)
                for g in range(2):
                    for h in range(2):
                        last = copy(k_hi[h * DH:(h + 1) * DH, br, g, :], work[g * DH:(g + 1) * DH, br, :])
                last.then_inc(k_hi_ready, 1)

            def odd_keys(c):
                act.wait_ge(pair_step, c + 1)
                act.wait_ge(proj_scaled, 3 + c)
                e = prob[:, c, :].rearrange("p (g t) -> p g t", g=2)
                copy(e[DH:P, :, 0:T - 1], e[0:DH, :, 1:T]).then_inc(odd_ready, 1)

            def split_values(br):
                act.wait_ge(aux_done, AUX.index("t_vs") + br + 1)
                copy(v_hi[:, br, :], ps_aux[:, :]).then_inc(v_hi_ready, 1)

            def split_blocks(c):
                act.wait_ge(blk_step, 4 * (c + 1))
                copy(pt_b[:, c, 0:2 * T], qf[:, c * 2 * T:(c + 1) * 2 * T]).then_inc(blk_hi_ready, 1)

            def tanh(c):
                act.wait_ge(gelu_in, c + 1)
                nc.scalar.activation(hid[:, 1, c, :], hid[:, 1, c, :], ACT.Tanh, scale=0.7978845608028654).then_inc(gelu_tanh, 1)

            def split_hidden(c):
                act.wait_ge(hid_ready, c + 1)
                copy(hid_hi[:, c, :], hid[:, 0, c, :]).then_inc(hid_hi_ready, 1)

            def kc_square():
                square_in = kcv[:, 0, :]
                act.wait_ge(aux_free, AUX.index("w2") + 1)
                nc.scalar.activation(kcm[:, 0, :], square_in, ACT.Square).then_inc(head_sq, 1)

            def kc_split():
                act.wait_ge(rope_ready, head_tiles("kc"))
                for g in range(2):
                    last = copy(kc_hi[:, g, :], kcv[:, 0, g * NCP:(g + 1) * NCP])
                last.then_inc(kc_hi_ready, 1)
                act.wait_ge(aux_done, AUX.index("t_vc") + 1)
                copy(vc_hi[:, :], ps_aux[0:NCP, 0:P]).then_inc(v_hi_ready, 1)

            sums_high(1)
            split(U_MIX + 2)
            root("x1", D)
            act.wait_ge(proj_scaled, 1)
            square("ks", sq[:, :], work[:, 0, :])
            split(U_MIX + 3)
            split(U_MIX + 4)
            root("ks", DH)
            act.wait_ge(proj_scaled, 2)
            square("kw", sq[:, :], work[:, 1, :])
            act.wait_ge(w2_landed, 32)
            copy(w2_hi[:, :, :], w2_raw[:, :, :, :].rearrange("p c g d -> p c (g d)")).then_inc(w2_hi_ready, 1)
            split(U_MIX + 5)
            root("kw", DH)
            odd_keys(0)
            split(U_MIX + 6)
            split_keys(0)
            odd_keys(1)
            split(U_W1)
            split_keys(1)
            split_blocks(0)
            split_values(0)
            split(U_W1 + 1)
            split_blocks(1)
            split_values(1)
            split(U_W1 + 2)
            split(U_W1 + 3)
            act.wait_ge(aux_done, AUX.index("t_gates") + 1)
            nc.scalar.activation(gate[:, 0, :], ps_aux[:, 0:NQ * 24], ACT.Exp, scale=-1.0).then_inc(gate_exp, 1)
            split(U_LOOP)
            tanh(0)
            split_hidden(0)
            split(U_LOOP + 1)
            tanh(1)
            split_hidden(1)

            def split_query(j, g):
                act.wait_ge(rope_ready, head_tiles("q0" if isinstance(j, int) and j == 0 else "q3"))
                at_least(act, qk_done, 8 * j - 4 + 4 * g)
                rows_ = slice(g * DH, (g + 1) * DH)
                copy(q_parts[rows_, g, :], qf[rows_, bass.ds(j * T, T)]).then_inc(qp_hi_ready, 1)

            def project_four(b, i):
                for u in range(4):
                    n = U_LOOP + 4 * b + u
                    if u == 2 and b:
                        kc_split()
                    if u == 1:
                        root("q3" if b else "q0", DH, i=i)
                    if not (u == 3 and b):
                        split(n + 2, i)
                    if u == 0:
                        if b:
                            root("kc", DH, 2 * NCP)
                        act.wait_ge(proj_scaled, 10 + 4 * b + 4 * i)
                        square("q3" if b else "q0", sq[:, :], work[:, 0, :], i)
                    if u == 2 and b:
                        split_query(0, 0)
                        split_query(0, 1)
                    if u == 3 and b:
                        nc.scalar.preload_act_table(ACT.Exp)
                        exps(0, 0)
                        exps_c(0, 0)
                    if u == 3:
                        act.wait_ge(ob_ready, b + i + 1)
                        copy(tile_of(ob_hi, b + i), work2[:, :]).then_inc(ob_hi_ready, 1)

            with act.Fori(0, 3) as i:
                project_four(0, i)
            def exps(j, s):
                j, s = j + s // 8, s % 8
                c = s % 4
                width = (c + 1) * P
                act.wait_ge(negmax_ready, 8 * j + s + 1)
                for br in range(2):
                    last = nc.scalar.activation(prob_of(s)[:, br * T:br * T + width], ps_s[:, 2 * (s % 2) + br, 0:width],
                                                ACT.Exp, bias=small[:, s % 2, br:br + 1], scale=DH ** -0.5,
                                                accum_out=small[:, s % 2, 2 + br:3 + br])
                last.then_inc(exp_done, 1)

            def exps_c(j, g):
                act.wait_ge(c_negmax_ready, 2 * j + g + 1)
                for c in range(NQ):
                    last = nc.scalar.activation(prob_c[:, c, :], ps_stat[:, c * NCP:(c + 1) * NCP], ACT.Exp,
                                                bias=small_c[:, 0, c:c + 1], scale=DH ** -0.5,
                                                accum_out=small_c[:, 1, c:c + 1])
                last.then_inc(c_exp_done, 1)

            def split_c(j, g):
                act.wait_ge(c_pt_done, 2 * j + g + 1)
                copy(ptc[:, 0, :], ps_stat[0:NCP, :]).then_inc(c_pt_hi_ready, 1)

            def split_probs(j, s):
                j, s = j + s // 8, s % 8
                c = s % 4
                pair = s // 2
                act.wait_ge(pt_done, 8 * j + s + 1)
                p_hi = turned_parts(pair % 2)[0].rearrange("p (b k h q) -> p b k h q", b=2, k=4, h=2)
                copy(p_hi[:, :, 0:c + 1, c % 2, :],
                     ps_y[:, :, 0:(c + 1) * P].rearrange("p b (k q) -> p b k q", q=P)).then_inc(pt_hi_ready, 1)

            def split_output(j, pair):
                j, pair = j + pair // 4, pair % 4
                act.wait_ge(pv_done, 4 * j + pair + 1)
                g, c = pair // 2, pair % 2
                rows_ = slice(g * DH, (g + 1) * DH)
                copy(xg_hi[rows_, bass.ds(j * T + c * 2 * P, 2 * P)],
                     ps_aux[rows_, c * 2 * P:(c + 1) * 2 * P]).then_inc(o_hi_ready, 1)

            def attend(j, first=False, last=False):
                for s in range(8):
                    if s % 2 == 0 and not (first and s <= 2):
                        split_output(j, (s - 4) // 2)
                    if not (first and s == 0):
                        split_probs(j, s - 1)
                    if not (last and s == 7):
                        exps(j, s + 1)
                    if s in (2, 6):
                        split_c(j, s // 4)
                    if s in (0, 4) and not (first and s == 0):
                        exps_c(j, s // 4)
                    if s in (3, 7) and not last:
                        split_query(j + 1, s // 4)
                    if first and s == 3:
                        split(U_OUT + 1)

            kc_square()
            project_four(3, 0)
            attend(0, first=True)
            with act.Fori(1, 3) as j:
                attend(j)
            attend(3, last=True)
            split_output(3, 2)
            split_probs(3, 7)
            split_output(3, 3)

            for d in range(KD):
                split(U_OUT + d + 2)
                if d < KD - 1:
                    take_x(2, d, R_FFN + 8 if d >= LATE else None)
            act.wait_ge(unit_done, U_OUT + KD)
            for d in range(LATE):
                xg_high(d, R_FFN + 8)
            take_x(2, KD - 1, R_FFN + 8)
            run_ffn(1, 2, 3, R_FFN + 16)
            run_ffn(2, 3, 4, R_MIX + KD)

            banks = [ps_s[:, 0, :], ps_s[:, 1, :], ps_s[:, 2, :], ps_s[:, 3, :], ps_y[:, 0, :], ps_y[:, 1, :],
                     ps_aux[:, :], ps_stat[:, :]]

            def take_product(u):
                act.wait_ge(unit_done, U_POOL + u + 1)
                for o in range(2):
                    d = 2 * POOL_ORDER[u] + o
                    last = nc.scalar.activation(h_pad[:, d, 16:TE], banks[2 * u + o], ACT.Copy,
                                                scale=cols[:, R_PSC + d:R_PSC + d + 1])
                last.then_inc(y_copied, 1)

            def gained_x(g):
                for d in (2 * g, 2 * g + 1):
                    act.wait_ge(x_ready, KD * 5 + d + 1)
                    xg_high(d, R_FFN + 24)

            def square_x(d):
                act.wait_ge(ss_step, KD * 5 + d - 1)
                nc.scalar.activation(square_of(d), tile_of(x_t, d), ACT.Square).then_inc(sq_ready, 1)

            nc.scalar.preload_act_table(ACT.Sqrt)
            split(U_POOL + 2)
            sums_high(4)
            take_product(0)
            root("x4", D)
            take_product(1)
            split(U_POOL + 3)
            take_product(2)
            split(U_POOL + 4)
            take_product(3)
            split(U_POOL + 5)
            gained_x(0)
            gained_x(1)
            square_x(0)
            square_x(1)
            gained_x(2)
            square_x(2)
            gained_x(3)
            for d in range(3, KD):
                square_x(d)
            run_ffn(3, 5, 6, None)

        @block.vector
        def _(dve):
            tt = nc.vector.tensor_tensor
            stt = nc.vector.scalar_tensor_tensor
            ts = nc.vector.tensor_scalar
            steps = [0]

            def then(ins):
                steps[0] += 1
                ins.then_inc(dve_step, 1)
                dve.wait_ge(dve_step, steps[0])

            def split(n, i=0):
                dve.wait_ge(hi_ready, n + 1 + 4 * i)
                size = BLOCKS[n] * P
                tt(w_lo[:, n % 2, 0:size], raw[:, n % 4, 0:size], f32(w_hi[:, n % 2, 0:size]),
                   ALU.subtract).then_inc(lo_ready, 1)

            def sums_low(version):
                dve.wait_ge(ss_hi_ready, version + 1)
                tt(ss_parts[:, 1, :], ss[:, :], f32(ss_parts[:, 0, :]), ALU.subtract).then_inc(ss_lo_ready, 1)

            def invert(name, dst, cols_=T, i=0):
                if name[0] != "x":
                    at_least(dve, gained, head_tiles(name) - 1 + i)
                dve.wait_ge(ms_ready, STATS.index(name) + i + 1)
                nc.vector.reciprocal(dst, ms[:, 0:cols_]).then_inc(root_ready, 1)

            def xg_low(version, d, gain):
                place = tile_order(2).index(d) if version == 2 else d
                dve.wait_ge(xg_hi_ready, KD * XG_OF[version] + place + 1)
                stt(tile_of(xg_lo, d), tile_of(x_t, d), cols[:, bass.ds(gain + d, 1)], f32(tile_of(xg_hi, d)),
                    ALU.mult, ALU.subtract).then_inc(xg_lo_ready, 1)

            def up(ffn, version, b, i, first=False):
                for u in range(4):
                    n, f = U_FFN[ffn] + 4 * b + u, 2 * (b + i) + u // 2
                    if first and u < 2:
                        if u == 0:
                            split(n + 3)
                    else:
                        split(n + 2, i)
                    dve.wait_ge(unit_done, n + 1 + 4 * i)
                    dve.wait_ge(root_ready, STATS.index(f"x{version}") + 1)
                    if u % 2 == 0:
                        tt(work[:, u // 2, :], ps_s[:, u // 2, :], rstd[:, :], ALU.mult).then_inc(gate_scaled, 1)
                    else:
                        a = work[:, u // 2, :]
                        tt(work2[:, :], ps_s[:, 2 + u // 2, :], rstd[:, :], ALU.mult).then_inc(up_scaled, 1)
                        dve.wait_ge(silu_ready, KF * ffn + f + 1)
                        dve.wait_ge(up_scaled, KF * ffn + f + 1)
                        tt(a, a, work2[:, :], ALU.mult).then_inc(a_ready, 1)
                        dve.wait_ge(act_hi_ready, KF * ffn + f + 1)
                        tt(tile_of(act_lo, f), a, f32(tile_of(act_hi, f)), ALU.subtract).then_inc(act_lo_ready, 1)

            def leave(d):
                dve.wait_ge(out_turned, d + 1)
                nc.vector.tensor_copy(out_rows[:, :, d * P:(d + 1) * P],
                                      ps_s[:, d % 4, :].rearrange("p (q f) -> p q f", q=NQ)).then_inc(out_copied, 1)

            def down(ffn, version_out, gain, b, i):
                for u in range(4):
                    n, d = U_FFN[ffn] + 2 * KF + 4 * b + u, 2 * (b + i) + u // 2
                    if n + 2 < U_END:
                        split(n + 2, i)
                    if u % 2:
                        dve.wait_ge(unit_done, n + 1 + 4 * i)
                        stt(tile_of(x_t, d), ps_y[:, u // 2, :], 0.5, tile_of(x_t, d), ALU.mult,
                            ALU.add).then_inc(x_ready, 1)
                        if gain is not None:
                            xg_low(version_out, d, gain)
                    if version_out == 6 and b:
                        for o in OUT_AFTER[u]:
                            leave(o)

            def run_ffn(ffn, version, version_out, gain):
                sums_low(version)
                split(U_FFN[ffn] + 2)
                invert(f"x{version}", rstd[:, :])
                up(ffn, version, 0, 0, first=True)
                with dve.Fori(1, KF // 2 - 1) as i:
                    up(ffn, version, 0, i)
                up(ffn, version, KF // 2 - 1, 0)
                with dve.Fori(0, KD // 2 - 1) as i:
                    down(ffn, version_out, gain, 0, i)
                down(ffn, version_out, gain, KD // 2 - 1, 0)

            nc.vector.memset(eps_col[:, :], EPS)
            then(nc.vector.memset(half[:, :], float(np.pi / 2)))
            dve.wait_ge(aux_done, 1)
            nc.vector.tensor_copy(cols[:, 0:R_MIX], ps_aux[:, 0:R_MIX]).then_inc(aux_free, 1)
            banks = [ps_s[:, 0, :], ps_s[:, 1, :], ps_s[:, 2, :], ps_s[:, 3, :], ps_y[:, 0, :], ps_y[:, 1, :],
                     ps_stat[:, :], ps_s[:, 1, :]]
            for d in range(KD):
                dve.wait_ge(x_turned, d + 1)
                nc.vector.tensor_copy(tile_of(x_t, d), banks[d]).then_inc(x_ready, 1)
                if d:
                    xg_low(0, d - 1, R_FFN)
                if d in (1, 3):
                    split(d // 2)
            xg_low(0, KD - 1, R_FFN)
            dve.wait_ge(pos_landed, 16)
            nc.vector.tensor_copy(pos_f[:, :], pos_i[:, :]).then_inc(pos_ready, 1)
            dve.wait_ge(aux_done, AUX.index("rows") + 1)
            nc.vector.tensor_copy(cols[:, R_MIX:N_ROWS], ps_aux[:, R_MIX:N_ROWS]).then_inc(aux_free, 1)
            dve.wait_ge(aux_done, AUX.index("pos") + 1)
            ts(ang, ps_aux[:, :], freq, None, ALU.mult).then_inc(aux_free, 1)
            run_ffn(0, 0, 1, R_MIX)

            def scaled(n, p, dst, src_rows=slice(0, P), i=0):
                dve.wait_ge(unit_done, n + 1 + 4 * i)
                bank = ps_y[:, 0, :] if p == LAST_P else ps_s[:, p % 4, :]
                tt(dst, bank[src_rows, :], rstd[src_rows, :], ALU.mult).then_inc(proj_scaled, 1)

            def gain_and_norm(name, gain, dst, cols_=T, i=0):
                dve.wait_ge(root_ready, STATS.index(name) + 1 + i)
                stt(dst, dst, cols[:, gain:gain + 1], ss[:, 0:cols_], ALU.mult, ALU.mult).then_inc(gained, 1)

            def rope(name, dst, i=0):
                dve.wait_ge(aux_done, AUX.index("rot_" + name) + 1 + i)
                dve.wait_ge(m1_ready, head_tiles(name) + i)
                tt(dst, ps_aux[:, :], sin_t[:, 0:T], ALU.mult).then_inc(aux_free, 1)
                dve.wait_ge(aux_free, AUX.index("rot_" + name) + 1 + i)
                tt(dst, dst, m1[:, :], ALU.add).then_inc(rope_ready, 1)

            def keys_low(br):
                dve.wait_ge(k_hi_ready, br + 1)
                for g in range(2):
                    rows_ = slice(g * DH, (g + 1) * DH)
                    for h in range(2):
                        last = tt(k_lo[h * DH:(h + 1) * DH, br, g, :], work[rows_, br, :], f32(k_hi[rows_, br, g, :]),
                                  ALU.subtract)
                last.then_inc(k_lo_ready, 1)

            def values_low(br):
                dve.wait_ge(v_hi_ready, br + 1)
                tt(v_lo[:, br, :], ps_aux[:, :], f32(v_hi[:, br, :]), ALU.subtract).then_inc(aux_free, 1)

            def pairs_of(n, p, c):
                dve.wait_ge(unit_done, n + 1)
                e = prob[:, c, :].rearrange("p (g t) -> p g t", g=2)
                for g in range(2):
                    rows_ = slice(g * DH, (g + 1) * DH)
                    tt(e[0:DH, g, 0:T], ps_s[rows_, p % 4, :], rstd[rows_, :],
                       ALU.mult).then_inc(proj_scaled if g else pair_step, 1)

            def gelu_argument(c):
                n, p = U_W1 + 2 * c + 1, 7 + c
                x, arg = hid[:, 0, c, :], hid[:, 1, c, :]
                dve.wait_ge(unit_done, n + 1)
                tt(x, ps_s[:, p % 4, 0:2 * NCP], ones[:, 0:2 * NCP], ALU.mult).then_inc(proj_scaled, 1)
                dve.wait_ge(proj_scaled, p + 1)
                then(tt(arg, x, x, ALU.mult))
                then(ts(arg, arg, 0.044715, 1.0, ALU.mult, ALU.add))
                tt(arg, arg, x, ALU.mult).then_inc(gelu_in, 1)

            def gelu_result(c):
                x, arg = hid[:, 0, c, :], hid[:, 1, c, :]
                dve.wait_ge(gelu_tanh, c + 1)
                then(stt(arg, arg, 1.0, x, ALU.add, ALU.mult))
                ts(x, arg, 0.5, None, ALU.mult).then_inc(hid_ready, 1)
                dve.wait_ge(hid_hi_ready, c + 1)
                tt(hid_lo[:, c, :], x, f32(hid_hi[:, c, :]), ALU.subtract).then_inc(hid_lo_ready, 1)

            sums_low(1)
            split(U_MIX + 2)
            invert("x1", rstd[:, :])
            dve.wait_ge(root_ready, STATS.index("x1") + 1)
            scaled(U_MIX, 0, work[:, 0, :])
            split(U_MIX + 3)
            scaled(U_MIX + 1, 1, work[:, 1, :])
            split(U_MIX + 4)
            invert("ks", ss[:, :])
            gain_and_norm("ks", R_KN + 1, work[:, 0, :])
            dve.wait_ge(mix_zeroed, 1)
            pairs_of(U_MIX + 2, 2, 0)
            split(U_MIX + 5)
            rope("ks", work[:, 0, :])
            invert("kw", ss[:, :])
            gain_and_norm("kw", R_KN + 2, work[:, 1, :])
            split(U_MIX + 6)
            pairs_of(U_MIX + 3, 3, 1)
            scaled(U_MIX + 4, 4, vt[:, :])
            rope("kw", work[:, 1, :])
            split(U_W1)
            dve.wait_ge(aux_done, AUX.index("t_vs") + 1)
            scaled(U_MIX + 5, 5, vt[:, :])
            values_low(0)
            split(U_W1 + 1)
            dve.wait_ge(aux_done, AUX.index("t_vw") + 1)
            scaled(U_MIX + 6, 6, vt[:, :])
            values_low(1)
            split(U_W1 + 2)
            keys_low(0)
            split(U_W1 + 3)
            gates_in = gate[:, 1, :]
            dve.wait_ge(gate_exp, 1)
            ts(gates_in, gate[:, 0, :], 1.0, None, ALU.add).then_inc(aux_free, 1)
            dve.wait_ge(aux_free, AUX.index("t_gates") + 1)
            then(nc.vector.reciprocal(gates_in, gates_in))
            cmp_gates = gate[:, 1, 0:24].rearrange("p (h b) -> p h b", b=3)[:, :, 0]
            then(ts(cmp_gates, cmp_gates, consts[:, C_VALID:C_VALID + 1], None, ALU.mult))
            split(U_LOOP)
            gelu_argument(0)
            gelu_result(0)
            keys_low(1)
            split(U_LOOP + 1)
            gelu_argument(1)
            gelu_result(1)
            dve.wait_ge(w2_hi_ready, 1)
            tt(w2_lo[:, :, :], w2_raw[:, :, :, :].rearrange("p c g d -> p c (g d)"), f32(w2_hi[:, :, :]),
               ALU.subtract).then_inc(w2_lo_ready, 1)

            def query_low(j, g):
                dve.wait_ge(qp_hi_ready, 2 * j + g + 1)
                rows_, other = slice(g * DH, (g + 1) * DH), slice((1 - g) * DH, (2 - g) * DH)
                tt(q_parts[other, g, :], qf[rows_, bass.ds(j * T, T)], f32(q_parts[rows_, g, :]),
                   ALU.subtract).then_inc(qp_lo_ready, 1)

            def project_four(b, i, extra=None):
                j = b + i
                name = "q3" if b else "q0"
                v, y = work[:, 1, :], vt[:, :]

                def conv_w(k):
                    return cols[:, bass.ds(R_CONV + 4 * k + j, 1)]

                for u in range(4):
                    n, p = U_LOOP + 4 * b + u, 9 + 4 * b + u
                    if u == 0:
                        scaled(n, p, work[:, 0, :], i=i)
                        split(n + 2, i)
                    if u == 1:
                        invert(name, ss[:, :], i=i)
                        gain_and_norm(name, R_QN, work[:, 0, :], i=i)
                        scaled(n, p, y, i=i)
                        if extra:
                            extra[1]()
                        split(n + 2, i)
                    if u == 2:
                        scaled(n, p, work2[:, :], i=i)
                        if extra:
                            extra[2]()
                        split(n + 2, i)
                        if b:
                            query_low(0, 0)
                            query_low(0, 1)
                        dve.wait_ge(proj_scaled, p + 1 + 4 * i)
                        tt(v, work2[:, :], y, ALU.mult).then_inc(conv_step, 1)
                        dve.wait_ge(conv_step, 4 * b + 1 + 4 * i)
                        ts(y, v, conv_w(2), None, ALU.mult).then_inc(conv_step, 1)
                        dve.wait_ge(conv_step, 4 * b + 2 + 4 * i)
                        stt(y[:, 1:T], v[:, 0:T - 1], conv_w(1), y[:, 1:T], ALU.mult, ALU.add).then_inc(conv_step, 1)
                        dve.wait_ge(conv_step, 4 * b + 3 + 4 * i)
                        stt(y[:, 2:T], v[:, 0:T - 2], conv_w(0), y[:, 2:T], ALU.mult, ALU.add).then_inc(conv_step, 1)
                    if u == 3:
                        rope(name, tile_of(qf, j), i)
                        if b:
                            maxima(0, 0)
                            maxima_c(0, 0)
                        scaled(n, p, work2[:, :], i=i)
                        if not b:
                            split(n + 2, i)
                        dve.wait_ge(proj_scaled, p + 1 + 4 * i)
                        dve.wait_ge(conv_step, 4 * b + 4 + 4 * i)
                        tt(work2[:, :], work2[:, :], y, ALU.mult).then_inc(ob_ready, 1)
                        dve.wait_ge(ob_hi_ready, j + 1)
                        tt(tile_of(ob_lo, j), work2[:, :], f32(tile_of(ob_hi, j)), ALU.subtract).then_inc(ob_lo_ready, 1)
                    if extra and u == 0:
                        extra[0]()

            with dve.Fori(0, 3) as i:
                project_four(0, i)

            def compressed():
                dve.wait_ge(aux_done, AUX.index("w2") + 1)
                tt(kcv[:, :, :].rearrange("p a b -> p (a b)"), ps_aux[:, 0:4 * NCP], ones[:, :],
                   ALU.mult).then_inc(aux_free, 1)

            def kc_norm():
                invert("kc", ss[:, 0:2 * NCP], 2 * NCP)
                gain_and_norm("kc", R_KN, kcv[:, 0, :], 2 * NCP)

            def kc_rope():
                dve.wait_ge(aux_done, AUX.index("rot_kc") + 1)
                dve.wait_ge(m1_ready, head_tiles("kc"))
                kc = kcv[:, 0, :]
                for g in range(2):
                    part = slice(g * NCP, (g + 1) * NCP)
                    s_at = sin_t[:, :].rearrange("p (n e) -> p n e", e=16)[:, 1:NCP + 1, 15]
                    last = tt(kc[:, part], ps_aux[:, part], s_at, ALU.mult)
                    if g == 0:
                        last.then_inc(dve_step, 1)
                        steps[0] += 1
                last.then_inc(aux_free, 1)
                dve.wait_ge(dve_step, steps[0])
                dve.wait_ge(aux_free, AUX.index("rot_kc") + 1)
                tt(kc, kc, kcm[:, 1, :], ALU.add).then_inc(rope_ready, 1)

            def kc_low():
                dve.wait_ge(kc_hi_ready, 1)
                tt(kc_lo[:, :, :].rearrange("p a b -> p (a b)"), kcv[:, 0, :],
                   f32(kc_hi[:, :, :].rearrange("p a b -> p (a b)")), ALU.subtract).then_inc(kc_ready, 1)
                dve.wait_ge(v_hi_ready, 3)
                tt(vc_lo[:, :], ps_aux[0:NCP, 0:P], f32(vc_hi[:, :]), ALU.subtract).then_inc(aux_free, 1)

            def maxima(j, s):
                j, s = j + s // 8, s % 8
                width = (s % 4 + 1) * P
                m = small[:, s % 2, :]
                dve.wait_ge(qk_done, 8 * j + s + 1)
                nc.vector.reduce_max(m[:, 8:10], ps_s[:, 2 * (s % 2):2 * (s % 2) + 2, 0:width], AX_X).then_inc(max_step, 1)
                dve.wait_ge(max_step, 8 * j + s + 1)
                ts(m[:, 0:2], m[:, 8:10], -DH ** -0.5, None, ALU.mult).then_inc(negmax_ready, 1)

            def maxima_c(j, g):
                dve.wait_ge(c_qk_done, 2 * j + g + 1)
                nc.vector.reduce_max(small_c[:, 4, :], ps_stat[:, 0:NQ * NCP].rearrange("p (c n) -> p c n", n=NCP),
                                     AX_X).then_inc(c_max_step, 1)
                dve.wait_ge(c_max_step, 2 * j + g + 1)
                ts(small_c[:, 0, :], small_c[:, 4, :], -DH ** -0.5, None, ALU.mult).then_inc(c_negmax_ready, 1)

            def scales_c(j, g):
                dve.wait_ge(c_exp_done, 2 * j + g + 1)
                nc.vector.reciprocal(small_c[:, 2, :], small_c[:, 1, :]).then_inc(c_sum_step, 1)
                dve.wait_ge(c_sum_step, 2 * j + g + 1)
                gates_c = gate[:, 1, :].rearrange("p (c x) -> p c x", c=NQ)[:, :, bass.ds(j * 3 + g * 12, 1)]
                tt(small_c[:, 3, :].unsqueeze(2), small_c[:, 2, :].unsqueeze(2), gates_c, ALU.mult).then_inc(c_scale_ready, 1)

            def probs_c_low(j, g):
                dve.wait_ge(c_pt_hi_ready, 2 * j + g + 1)
                tt(ptc[:, 1, :], ps_stat[0:NCP, :], f32(ptc[:, 0, :]), ALU.subtract).then_inc(c_pt_lo_ready, 1)

            def scales(j, s):
                g, c = s // 4, s % 4
                m = small[:, s % 2, :]
                dve.wait_ge(exp_done, 8 * j + s + 1)
                nc.vector.reciprocal(m[:, 4:6], m[:, 2:4]).then_inc(sum_step, 1)
                dve.wait_ge(sum_step, 8 * j + s + 1)
                for br in range(2):
                    last = ts(diagonal(s, br), ident, m[:, 4 + br:5 + br],
                              gate[:, 1, bass.ds(j * 3 + c * 24 + g * 12 + 1 + br, 1)], ALU.mult, ALU.mult)
                last.then_inc(scale_ready, 1)

            def probs_low(j, s):
                j, s = j + s // 8, s % 8
                c, pair = s % 4, s // 2
                dve.wait_ge(pt_hi_ready, 8 * j + s + 1)
                p_hi, p_lo = (x.rearrange("p (b k h q) -> p b k h q", b=2, k=4, h=2)[:, :, 0:c + 1, c % 2, :]
                              for x in turned_parts(pair % 2))
                tt(p_lo, ps_y[:, :, 0:(c + 1) * P].rearrange("p b (k q) -> p b k q", q=P), f32(p_hi),
                   ALU.subtract).then_inc(pt_lo_ready, 1)

            def output_low(j, pair):
                j, pair = j + pair // 4, pair % 4
                dve.wait_ge(o_hi_ready, 4 * j + pair + 1)
                g, c = pair // 2, pair % 2
                rows_, at = slice(g * DH, (g + 1) * DH), bass.ds(j * T + c * 2 * P, 2 * P)
                tt(xg_lo[rows_, at], ps_aux[rows_, c * 2 * P:(c + 1) * 2 * P], f32(xg_hi[rows_, at]),
                   ALU.subtract).then_inc(o_lo_ready, 1)

            def attend(j, first=False, last=False):
                for s in range(8):
                    if not (last and s == 7):
                        maxima(j, s + 1)
                    scales(j, s)
                    if s % 2 == 0 and not (first and s <= 2):
                        output_low(j, (s - 4) // 2)
                    if not (first and s == 0):
                        probs_low(j, s - 1)
                    if s in (2, 6):
                        probs_c_low(j, s // 4)
                    if s in (0, 4) and not (first and s == 0):
                        maxima_c(j, s // 4)
                    if s in (1, 5) and not (first and s == 1):
                        scales_c(j, s // 4)
                    if s in (3, 7) and not last:
                        query_low(j + 1, s // 4)
                    if first and s == 3:
                        split(U_OUT + 1)

            compressed()
            project_four(3, 0, {0: kc_norm, 1: kc_rope, 2: kc_low})
            scales_c(0, 0)
            attend(0, first=True)
            with dve.Fori(1, 3) as j:
                attend(j)
            attend(3, last=True)
            output_low(3, 2)
            probs_low(3, 7)
            output_low(3, 3)

            for d in range(KD):
                split(U_OUT + d + 2)
                dve.wait_ge(unit_done, U_OUT + d + 1)
                tt(tile_of(x_t, d), ps_s[:, 2 + d % 2, :], tile_of(x_t, d), ALU.add).then_inc(x_ready, 1)
                if LATE <= d < KD - 1:
                    xg_low(2, d, R_FFN + 8)
            for d in (*range(LATE), KD - 1):
                xg_low(2, d, R_FFN + 8)
            run_ffn(1, 2, 3, R_FFN + 16)
            run_ffn(2, 3, 4, R_MIX + KD)

            def pool_group(g, meanwhile=None):
                dve.wait_ge(y_copied, POOL_ORDER.index(g) + 1)
                z = normed(tt, g)
                if g == 2:
                    z.then_inc(z_ready, 1)
                    dve.wait_ge(z_ready, 1)
                else:
                    then(z)
                if meanwhile is not None:
                    split(meanwhile)
                total = window_sum(tt, then, g, sums_v)
                if g == 2:
                    dve.wait_ge(less_z, 2)
                elif g == 1:
                    then(x_less_z(tt, g))
                add_mean(g, total)

            def add_mean(g, total):
                for o in range(2):
                    x = tile_of(x_t, 2 * g + o)
                    stt(x, total[:, o, 16:TE], 1.0 / (2 << g), x, ALU.mult, ALU.add).then_inc(x_ready, 1)

            def lows(g):
                for d in (2 * g, 2 * g + 1):
                    xg_low(5, d, R_FFN + 24)

            split(U_POOL + 2)
            sums_low(4)
            invert("x4", rstd[:, :])
            dve.wait_ge(root_ready, STATS.index("x4") + 1)
            dve.wait_ge(pool_zeroed, 1)
            pool_group(0, meanwhile=U_POOL + 3)
            split(U_POOL + 4)
            pool_group(1)
            lows(0)
            split(U_POOL + 5)
            pool_group(2)
            lows(1)
            dve.wait_ge(less_z, 1)
            add_mean(3, sums_p[1])
            lows(2)
            lows(3)
            for d in range(KD // 2, KD):
                dve.wait_ge(sq_ready, KD * 5 + d + 1)
                dve.wait_ge(ss_step, KD * 5 + d)
                tt(ss[:, :], ss[:, :], square_of(d), ALU.add).then_inc(ss_step, 1)
            run_ffn(3, 5, 6, None)

        @block.gpsimd
        def _(pool):
            tt = nc.gpsimd.tensor_tensor
            ts = nc.gpsimd.tensor_scalar
            steps = [0]

            def then(ins):
                steps[0] += 1
                ins.then_inc(pool_step, 1)
                pool.wait_ge(pool_step, steps[0])

            def sums(version, tiles=KD):
                for d in range(tiles):
                    pool.wait_ge(sq_ready, KD * version + d + 1)
                    if d == 0:
                        at_least(pool, stat_done, STATS.index(f"x{version}"))
                        nc.gpsimd.tensor_copy(ss[:, :], square_of(d)).then_inc(ss_step, 1)
                    else:
                        pool.wait_ge(ss_step, KD * version + d)
                        tt(ss[:, :], ss[:, :], square_of(d), ALU.add).then_inc(ss_step, 1)

            def cosine(name, slot_, i=0):
                pool.wait_ge(gained, head_tiles(name) + i)
                at_least(pool, rope_ready, head_tiles(name) - 1 + i)
                tt(m1[:, :], work[:, slot_, :], cos_t[:, 0:T], ALU.mult).then_inc(m1_ready, 1)

            nc.gpsimd.memset(sin_t[:, T:TE], 0.0)
            then(nc.gpsimd.memset(cos_t[:, T:TE], 0.0))
            sums(0)

            pool.wait_ge(aux_free, AUX.index("pos") + 1)
            pool.wait_ge(stat_done, 1)
            for many in (1024.0, 1.0):
                then(ts(turns, ang, 1.0 / (2 * np.pi * many), ROUND, ALU.mult, ALU.add))
                then(ts(turns, turns, ROUND, None, ALU.subtract))
                for part in PI_PARTS:
                    then(ts(step_, turns, part * many, None, ALU.mult))
                    then(tt(ang, ang, step_, ALU.subtract))
            ts(ang, ang, 3.1415925, -3.1415925, ALU.min, ALU.max).then_inc(turn_ready, 1)

            sums(1)
            nc.gpsimd.memset(prob[:, :, :].rearrange("p c (g t) -> p c g t", g=2)[:, :, :, T - 1:TE], 0.0).then_inc(mix_zeroed, 1)
            pool.wait_ge(trig_ready, 3)
            def blocks(c):
                pool.wait_ge(proj_scaled, 3 + c)
                pool.wait_ge(odd_ready, c + 1)
                e = prob[:, c, :].rearrange("p (g m b e) -> p g b m e", g=2, b=8, e=2)
                dst = qf[:, c * 2 * T:(c + 1) * 2 * T].rearrange("p (j g n) -> p g j n", g=2, n=NCP)
                for g in range(2):
                    for a in range(2):
                        at = R_POS + 16 * c + 8 * a
                        tt(dst[:, g, 8 * a:8 * a + 8, :], e[:, g, :, a:a + NCP, 0],
                           cols[:, at:at + 8].unsqueeze(2).to_broadcast([P, 8, NCP]), ALU.add).then_inc(blk_step, 1)

            def blocks_low(c):
                pool.wait_ge(blk_step, 4 * (c + 1))
                pool.wait_ge(blk_hi_ready, c + 1)
                tt(pt_b[:, c, 2 * T:4 * T], qf[:, c * 2 * T:(c + 1) * 2 * T], f32(pt_b[:, c, 0:2 * T]),
                   ALU.subtract).then_inc(blk_lo_ready, 1)

            cosine("ks", 0)
            blocks(0)
            cosine("kw", 1)
            blocks(1)
            blocks_low(0)
            blocks_low(1)
            with pool.Fori(0, 3) as i:
                cosine("q0", 0, i)
            pool.wait_ge(gained, head_tiles("kc"))
            for g in range(2):
                part = slice(g * NCP, (g + 1) * NCP)
                c_at = cos_t[:, :].rearrange("p (n e) -> p n e", e=16)[:, 1:NCP + 1, 15]
                last = tt(kcm[:, 1, part], kcv[:, 0, part], c_at, ALU.mult)
            last.then_inc(m1_ready, 1)
            cosine("q3", 0)

            pool.wait_ge(unit_done, U_OUT)
            for slot_ in range(2):
                for part in turned_parts(slot_):
                    zeros = part.rearrange("p (b k h q) -> p b k h q", b=2, k=4, h=2)[:, :, 2 * slot_ + 1, 0, :]
                    last = tt(zeros, consts[:, 0:2 * P].rearrange("p (b q) -> p b q", b=2),
                              consts[:, 0:2 * P].rearrange("p (b q) -> p b q", b=2), ALU.subtract)
            last.then_inc(probs_zeroed, 1)
            with pool.Fori(0, 8) as head:
                pool.wait_ge(c_scale_ready, head + 1)
                tt(prob_c[:, :, :], prob_c[:, :, :], small_c[:, 3, :].unsqueeze(2).to_broadcast([P, NQ, NCP]),
                   ALU.mult).then_inc(c_p_scaled, 1)

            for version in (2, 3, 4):
                sums(version)
            for pad in (h_pad, *sums_v, *sums_p):
                last = nc.gpsimd.memset(pad[:, :, 0:16], 0.0)
            last.then_inc(pool_zeroed, 1)
            pool.wait_ge(pool_zeroed, 1)
            pool.wait_ge(root_ready, STATS.index("x4") + 1)
            pool.wait_ge(y_copied, POOL_ORDER.index(3) + 1)
            then(normed(tt, 3))
            window_sum(tt, then, 3, sums_p)
            x_less_z(tt, 3).then_inc(less_z, 1)
            pool.wait_ge(z_ready, 1)
            x_less_z(tt, 2).then_inc(less_z, 1)
            sums(5, KD // 2)


_INS = ["x", "positions", "ffn_norm", "ffn_w_gate", "ffn_w_up", "ffn_w_down", "mix_norm", "hyb_w_in", "hyb_q_norm",
        "hyb_k_norm", "hyb_cmp_pos", "hyb_cmp_w1", "hyb_cmp_w2", "hyb_conv_w", "hyb_w_out", "pool_w", "pool_scale"]


def kernel(**inputs):
    import concourse.bacc as bacc
    from concourse.bass_utils import run_bass_kernel_spmd as run

    nc = bacc.Bacc("TRN2", target_bir_lowering=False, num_devices=1)
    arrays, aps = {}, {}
    for name in _INS + ["consts"]:
        a = shape_constants() if name == "consts" else np.ascontiguousarray(inputs[name])
        arrays[f"in_{name}"] = a
        aps[name] = nc.dram_tensor(f"in_{name}", a.shape, mybir.dt.from_np(a.dtype), kind="ExternalInput").ap()
    out = nc.dram_tensor("out_0", (1, T, D), F32, kind="ExternalOutput").ap()
    build(nc, aps, out)
    return run(nc, [arrays], core_ids=[0]).results[0]["out_0"]
```
